# Optimizing a Trainium2 kernel written in Bass

```python
import jax, jax.numpy as jnp
from jax import lax
import numpy as np

D_MODEL = 1024
BATCH = 1
SEQ = 512
DEPTH = 1

CHUNK = 64
N_LEFT_CHUNKS = 8
BAND = (N_LEFT_CHUNKS + 1) * CHUNK
ATT_HEADS = 8
ATT_HEAD_DIM = 64
D_ATT = ATT_HEADS * ATT_HEAD_DIM
D_CONV = D_MODEL // 2
CONV_WIDTH = 3
MAX_REL = 128
N_REL = 2 * MAX_REL + 1
EPS = 1e-6
NEG_BIG = -1e30
IN_SIZES = (D_ATT, D_ATT, D_ATT, D_ATT, D_CONV, D_CONV, D_CONV, D_CONV, D_MODEL, D_MODEL)
IN_COLS = sum(IN_SIZES)
IN_SPLITS = tuple(int(s) for s in np.cumsum(IN_SIZES)[:-1])


def rmsnorm(x, g):
    xf = x.astype(jnp.float32)
    r = lax.rsqrt(jnp.mean(xf * xf, axis=-1, keepdims=True) + EPS)
    return (xf * r).astype(x.dtype) * g

def chunked_rel_attention(q, k, v, rel_bias):
    b, s, h, dh = q.shape
    nc = s // CHUNK
    qc = q.reshape(b, nc, CHUNK, h, dh)
    kc = k.reshape(b, nc, CHUNK, h, dh)
    vc = v.reshape(b, nc, CHUNK, h, dh)
    pad = ((0, 0), (N_LEFT_CHUNKS, 0), (0, 0), (0, 0), (0, 0))
    kp = jnp.pad(kc, pad)
    vp = jnp.pad(vc, pad)
    kb = jnp.concatenate([kp[:, j:j + nc] for j in range(N_LEFT_CHUNKS + 1)], axis=2)
    vb = jnp.concatenate([vp[:, j:j + nc] for j in range(N_LEFT_CHUNKS + 1)], axis=2)
    scale = ATT_HEAD_DIM ** -0.5
    scores = jnp.einsum('bcqhd,bckhd->bhcqk', qc, kb).astype(jnp.float32) * scale
    rel = np.arange(CHUNK)[:, None] + N_LEFT_CHUNKS * CHUNK - np.arange(BAND)[None, :]
    idx = np.clip(rel, -MAX_REL, MAX_REL) + MAX_REL
    bias = rel_bias[:, idx].astype(jnp.float32)
    kpos = np.arange(nc)[:, None] * CHUNK - N_LEFT_CHUNKS * CHUNK + np.arange(BAND)[None, :]
    valid = jnp.asarray(kpos >= 0)
    scores = jnp.where(valid[None, None, :, None, :], scores + bias[None, :, None], NEG_BIG)
    p = jax.nn.softmax(scores, axis=-1).astype(v.dtype)
    out = jnp.einsum('bhcqk,bckhd->bcqhd', p, vb)
    return out.reshape(b, s, h * dh)

def causal_depthwise_conv(u, w, bias):
    s = u.shape[1]
    up = jnp.pad(u, ((0, 0), (CONV_WIDTH - 1, 0), (0, 0)))
    return sum(w[t] * up[:, t:t + s] for t in range(CONV_WIDTH)) + bias

def first_inputs(seed: int = 0) -> dict:
    key = jax.random.key(seed)
    ks = jax.random.split(key, 12)
    f32 = jnp.float32
    x = jax.random.normal(ks[0], (BATCH, SEQ, D_MODEL), f32)
    norm_g = 1.0 + 0.05 * jax.random.normal(ks[1], (DEPTH, D_MODEL), f32)
    w_in = jax.random.normal(ks[2], (DEPTH, D_MODEL, IN_COLS), f32) * D_MODEL ** -0.5
    rel_bias = 0.2 * jax.random.normal(ks[3], (DEPTH, ATT_HEADS, N_REL), f32)
    w_att_out = jax.random.normal(ks[4], (DEPTH, D_ATT, D_MODEL), f32) * D_ATT ** -0.5
    conv_w = jax.random.normal(ks[5], (DEPTH, CONV_WIDTH, D_CONV), f32) * CONV_WIDTH ** -0.5
    conv_b = 0.02 * jax.random.normal(ks[6], (DEPTH, D_CONV), f32)
    w_conv_out = jax.random.normal(ks[7], (DEPTH, D_CONV, D_MODEL), f32) * D_CONV ** -0.5
    w_out = jax.random.normal(ks[8], (DEPTH, D_MODEL, D_MODEL), f32) * D_MODEL ** -0.5
    final_norm_g = 1.0 + 0.05 * jax.random.normal(ks[9], (D_MODEL,), f32)
    return {"x": x, "norm_g": norm_g, "w_in": w_in, "rel_bias": rel_bias,
            "w_att_out": w_att_out, "conv_w": conv_w, "conv_b": conv_b,
            "w_conv_out": w_conv_out, "w_out": w_out, "final_norm_g": final_norm_g}

def first_block(x, norm_g, w_in, rel_bias, w_att_out, conv_w, conv_b, w_conv_out, w_out, final_norm_g):
    b, s, _ = x.shape
    for l in range(DEPTH):
        h = rmsnorm(x, norm_g[l])
        proj = jnp.einsum('bsd,de->bse', h, w_in[l])
        q, k, v, z_att, gb, gc, u, z_conv, g_att, g_conv = jnp.split(proj, IN_SPLITS, axis=-1)
        att = chunked_rel_attention(q.reshape(b, s, ATT_HEADS, ATT_HEAD_DIM),
                                    k.reshape(b, s, ATT_HEADS, ATT_HEAD_DIM),
                                    v.reshape(b, s, ATT_HEADS, ATT_HEAD_DIM),
                                    rel_bias[l])
        y_att = jnp.einsum('bsc,cd->bsd', att * jax.nn.silu(z_att), w_att_out[l])
        vconv = causal_depthwise_conv(gc * u, conv_w[l], conv_b[l])
        y_conv = jnp.einsum('bsc,cd->bsd', gb * vconv * jax.nn.silu(z_conv), w_conv_out[l])
        m = jax.nn.sigmoid(g_att) * y_att + jax.nn.sigmoid(g_conv) * y_conv
        x = x + jnp.einsum('bsd,de->bse', m, w_out[l])
    return rmsnorm(x, final_norm_g)


DEPTH_2 = 2

HEAD_DIM = 128
N_HEADS_A = 4
A_WIDTH = N_HEADS_A * HEAD_DIM
IDX_HEADS = 8
IDX_DIM = 64
IDX_TOPK_MAX = 256
N_HEADS_B = 4
GLA_DK = 64
GLA_DV = 128
GLA_GATE_RANK = 16
GLA_TAU = 16.0
B_WIDTH = N_HEADS_B * GLA_DV
N_HEADS_C = 8
C_WIDTH = N_HEADS_C * HEAD_DIM
SB_QBLOCK = 128
ROPE_THETA = 500000.0
ROPE_FRACTION = 4
D_FF = 4 * D_MODEL
N_EVEN = (DEPTH_2 + 1) // 2
N_ODD = DEPTH_2 // 2
AB_SIZES = (
    A_WIDTH, A_WIDTH, A_WIDTH,
    IDX_HEADS * IDX_DIM, IDX_DIM, IDX_HEADS,
    N_HEADS_B * GLA_DK, N_HEADS_B * GLA_DK,
    B_WIDTH,
    GLA_GATE_RANK,
    B_WIDTH,
)
AB_PROJ = sum(AB_SIZES)


def _split(a, sizes):
    out, o = [], 0
    for s in sizes:
        out.append(a[..., o:o + s])
        o += s
    return out

def rmsnorm_2(x, g):
    xf = x.astype(jnp.float32)
    y = xf * lax.rsqrt(jnp.mean(xf * xf, axis=-1, keepdims=True) + EPS)
    return (y * g.astype(jnp.float32)).astype(x.dtype)

def rope_partial(x, pos):
    d = x.shape[-1]
    rot = d // ROPE_FRACTION
    half = rot // 2
    inv = jnp.power(ROPE_THETA, -jnp.arange(half, dtype=jnp.float32) * 2.0 / rot)
    ang = pos.astype(jnp.float32)[:, None] * inv[None, :]
    cos = jnp.cos(ang)[None, :, None, :]
    sin = jnp.sin(ang)[None, :, None, :]
    xf = x.astype(jnp.float32)
    x1, x2, rest = xf[..., :half], xf[..., half:rot], xf[..., rot:]
    out = jnp.concatenate([x1 * cos - x2 * sin, x2 * cos + x1 * sin, rest], axis=-1)
    return out.astype(x.dtype)

def dsa_attention(q, k, v, iq, ik, iw):
    bsz, s_len, n_h, d_h = q.shape
    topk = min(IDX_TOPK_MAX, s_len // 4)
    n_blk = s_len // CHUNK
    key_pos = jnp.arange(s_len)

    def blk_fn(args):
        c, qb, iqb, iwb = args
        logits = jnp.einsum('bthd,bsd->bths', iqb, ik).astype(jnp.float32) * IDX_DIM ** -0.5
        score = jnp.einsum('bths,bth->bts', jax.nn.relu(logits),
                           iwb.astype(jnp.float32) * IDX_HEADS ** -0.5)
        limit = (c + 1) * CHUNK
        score = jnp.where((key_pos < limit)[None, None, :], score, -jnp.inf)
        _, idx = lax.top_k(score, topk)
        valid = idx < limit
        ks = jax.vmap(lambda a, i: a[i])(k, idx)
        vs = jax.vmap(lambda a, i: a[i])(v, idx)
        s = jnp.einsum('bthd,btkhd->bthk', qb, ks).astype(jnp.float32) * HEAD_DIM ** -0.5
        s = jnp.where(valid[:, :, None, :], s, -jnp.inf)
        p = jax.nn.softmax(s, axis=-1)
        return jnp.einsum('bthk,btkhd->bthd', p.astype(v.dtype), vs)

    def to_blocks(a):
        return a.reshape(bsz, n_blk, CHUNK, *a.shape[2:]).swapaxes(0, 1)

    out = lax.map(blk_fn, (jnp.arange(n_blk), to_blocks(q), to_blocks(iq), to_blocks(iw)))
    return out.swapaxes(0, 1).reshape(bsz, s_len, n_h, d_h)

def gla_chunked(q, k, v, lg):
    bsz, s_len, n_h, dk = q.shape
    dv = v.shape[-1]
    n_c = s_len // CHUNK
    causal = jnp.tril(jnp.ones((CHUNK, CHUNK), dtype=bool))

    def chunks(a):
        return a.astype(jnp.float32).reshape(bsz, n_c, CHUNK, n_h, a.shape[-1]).transpose(1, 0, 3, 2, 4)

    def step(state, inp):
        qc, kc, vc, gc = inp
        b = jnp.cumsum(gc, axis=2)
        o_inter = jnp.einsum('bhtd,bhde->bhte', qc * jnp.exp(b), state)
        diff = b[:, :, :, None, :] - b[:, :, None, :, :]
        decay = jnp.exp(jnp.where(causal[:, :, None], diff, -jnp.inf))
        att = jnp.einsum('bhtd,bhsd,bhtsd->bhts', qc, kc, decay)
        o = o_inter + jnp.einsum('bhts,bhse->bhte', att, vc)
        b_last = b[:, :, -1:, :]
        state = (jnp.exp(b_last[:, :, 0, :])[..., None] * state
                 + jnp.einsum('bhsd,bhse->bhde', kc * jnp.exp(b_last - b), vc))
        return state, o

    s0 = jnp.zeros((bsz, n_h, dk, dv), jnp.float32)
    _, o = lax.scan(step, s0, (chunks(q), chunks(k), chunks(v), chunks(lg)))
    return o.transpose(1, 0, 3, 2, 4).reshape(bsz, s_len, n_h, dv)

def stick_breaking(q, k, v):
    bsz, s_len, n_h, d_h = q.shape
    n_blk = s_len // SB_QBLOCK
    key_pos = jnp.arange(s_len)

    def blk_fn(args):
        i, qb = args
        z = jnp.einsum('bthd,bshd->bhts', qb, k).astype(jnp.float32) * d_h ** -0.5
        t_pos = i * SB_QBLOCK + jnp.arange(SB_QBLOCK)
        mask = key_pos[None, :] < t_pos[:, None]
        lo = jnp.where(mask, jax.nn.log_sigmoid(-z), 0.0)
        rc = lax.cumsum(lo, axis=3, reverse=True)
        log_a = jax.nn.log_sigmoid(z) + (rc - lo)
        a = jnp.where(mask, jnp.exp(log_a), 0.0)
        return jnp.einsum('bhts,bshd->bthd', a.astype(v.dtype), v)

    qb = q.reshape(bsz, n_blk, SB_QBLOCK, n_h, d_h).swapaxes(0, 1)
    out = lax.map(blk_fn, (jnp.arange(n_blk), qb))
    return out.swapaxes(0, 1).reshape(bsz, s_len, n_h, d_h)

def mixer_ab(n, pos, w_in, gq, gk, w_gate_up, b_gate, g_gla, w_out):
    bsz, s_len, _ = n.shape
    proj = n @ w_in
    (qa, ka, va, iq, ik, iw, qb, kb, vb, g_low, og) = _split(proj, AB_SIZES)
    qa = rope_partial(rmsnorm_2(qa.reshape(bsz, s_len, N_HEADS_A, HEAD_DIM), gq), pos)
    ka = rope_partial(rmsnorm_2(ka.reshape(bsz, s_len, N_HEADS_A, HEAD_DIM), gk), pos)
    va = va.reshape(bsz, s_len, N_HEADS_A, HEAD_DIM)
    iq = rope_partial(iq.reshape(bsz, s_len, IDX_HEADS, IDX_DIM), pos)
    ik = rope_partial(ik[:, :, None, :], pos)[:, :, 0, :]
    oa = dsa_attention(qa, ka, va, iq, ik, iw).reshape(bsz, s_len, A_WIDTH)
    qb = qb.reshape(bsz, s_len, N_HEADS_B, GLA_DK) * GLA_DK ** -0.5
    kb = kb.reshape(bsz, s_len, N_HEADS_B, GLA_DK)
    vb = vb.reshape(bsz, s_len, N_HEADS_B, GLA_DV)
    gate = (g_low @ w_gate_up + b_gate).astype(jnp.float32)
    lg = (jax.nn.log_sigmoid(gate) / GLA_TAU).reshape(bsz, s_len, N_HEADS_B, GLA_DK)
    ob = gla_chunked(qb, kb, vb, lg).astype(n.dtype)
    ob = rmsnorm_2(ob, g_gla).reshape(bsz, s_len, B_WIDTH) * jax.nn.silu(og)
    return jnp.concatenate([oa, ob], axis=-1) @ w_out

def mixer_c(n, w_in, gq, gk, w_out):
    bsz, s_len, _ = n.shape
    q, k, v = _split(n @ w_in, (C_WIDTH, C_WIDTH, C_WIDTH))
    q = rmsnorm_2(q.reshape(bsz, s_len, N_HEADS_C, HEAD_DIM), gq)
    k = rmsnorm_2(k.reshape(bsz, s_len, N_HEADS_C, HEAD_DIM), gk)
    v = v.reshape(bsz, s_len, N_HEADS_C, HEAD_DIM)
    return stick_breaking(q, k, v).reshape(bsz, s_len, C_WIDTH) @ w_out

def squared_relu_mlp(n, w_up, w_down):
    return jnp.square(jax.nn.relu(n @ w_up)) @ w_down

def second_inputs(seed: int = 0) -> dict:
    key = jax.random.key(seed)
    ks = jax.random.split(key, 16)
    f32 = jnp.float32

    def w(k, shape, fan_in):
        return jax.random.normal(k, shape, f32) * fan_in ** -0.5

    def gain(k, shape):
        return 1.0 + 0.02 * jax.random.normal(k, shape, f32)

    return {
        "x": jax.random.normal(ks[0], (BATCH, SEQ, D_MODEL), f32),
        "g_mix": gain(ks[1], (DEPTH_2, D_MODEL)),
        "g_ffn": gain(ks[2], (DEPTH_2, D_MODEL)),
        "w_in_ab": w(ks[3], (N_EVEN, D_MODEL, AB_PROJ), D_MODEL),
        "gq_a": gain(ks[4], (N_EVEN, HEAD_DIM)),
        "gk_a": gain(ks[5], (N_EVEN, HEAD_DIM)),
        "w_gate_up": w(ks[6], (N_EVEN, GLA_GATE_RANK, N_HEADS_B * GLA_DK), GLA_GATE_RANK),
        "b_gate": 0.1 * jax.random.normal(ks[7], (N_EVEN, N_HEADS_B * GLA_DK), f32),
        "g_gla": gain(ks[8], (N_EVEN, GLA_DV)),
        "w_out_ab": w(ks[9], (N_EVEN, A_WIDTH + B_WIDTH, D_MODEL), A_WIDTH + B_WIDTH),
        "w_in_c": w(ks[10], (N_ODD, D_MODEL, 3 * C_WIDTH), D_MODEL),
        "gq_c": gain(ks[11], (N_ODD, HEAD_DIM)),
        "gk_c": gain(ks[12], (N_ODD, HEAD_DIM)),
        "w_out_c": w(ks[13], (N_ODD, C_WIDTH, D_MODEL), C_WIDTH),
        "w_up": w(ks[14], (DEPTH_2, D_MODEL, D_FF), D_MODEL),
        "w_down": w(ks[15], (DEPTH_2, D_FF, D_MODEL), D_FF),
    }

def second_block(x, g_mix, g_ffn, w_in_ab, gq_a, gk_a, w_gate_up, b_gate, g_gla, w_out_ab,
              w_in_c, gq_c, gk_c, w_out_c, w_up, w_down):
    pos = jnp.arange(x.shape[1])
    h = x
    for layer in range(DEPTH_2):
        n = rmsnorm_2(h, g_mix[layer])
        if layer % 2 == 0:
            i = layer // 2
            h = h + mixer_ab(n, pos, w_in_ab[i], gq_a[i], gk_a[i], w_gate_up[i],
                             b_gate[i], g_gla[i], w_out_ab[i])
        else:
            i = layer // 2
            h = h + mixer_c(n, w_in_c[i], gq_c[i], gk_c[i], w_out_c[i])
        h = h + squared_relu_mlp(rmsnorm_2(h, g_ffn[layer]), w_up[layer], w_down[layer])
    return h


def setup_inputs(seed=0):
    out = dict(first_inputs(seed))
    for name, value in second_inputs(seed + 1).items():
        if name != "x":
            out[name + "_2"] = value
    return out


def reference(
    x, norm_g, w_in, rel_bias, w_att_out, conv_w, conv_b, w_conv_out, w_out, final_norm_g,
    g_mix_2, g_ffn_2, w_in_ab_2, gq_a_2, gk_a_2, w_gate_up_2, b_gate_2, g_gla_2, w_out_ab_2,
    w_in_c_2, gq_c_2, gk_c_2, w_out_c_2, w_up_2, w_down_2,
):
    x = first_block(
        x, norm_g, w_in, rel_bias, w_att_out, conv_w, conv_b, w_conv_out, w_out, final_norm_g,
    )
    return second_block(
        x, g_mix_2, g_ffn_2, w_in_ab_2, gq_a_2, gk_a_2, w_gate_up_2, b_gate_2, g_gla_2,
        w_out_ab_2, w_in_c_2, gq_c_2, gk_c_2, w_out_c_2, w_up_2, w_down_2,
    )


_drawn_inputs = setup_inputs


def setup_inputs(seed=0):
    import zlib

    import numpy as np

    out = dict(_drawn_inputs(seed))
    spreads = {}
    factors = {'rel_bias': 4.642,
     'conv_b': 4.54,
     'gq_a_2': 8.0,
     'gk_a_2': 8.0,
     'b_gate_2': 2.978,
     'g_gla_2': 6.639,
     'gq_c_2': 8.0,
     'gk_c_2': 8.0}
    for name, (base, spread) in spreads.items():
        noise = np.random.default_rng([zlib.crc32(name.encode()), seed]).standard_normal(out[name].shape)
        drawn = base * np.exp(spread * noise) if base else spread * noise
        out[name] = __import__('jax').numpy.asarray(drawn.astype(out[name].dtype))
    for name, factor in factors.items():
        out[name] = (out[name] * factor).astype(out[name].dtype)
    return out
```

```python
from contextlib import ExitStack

import numpy as np
import concourse.bass as bass
from concourse import mybir

P = 128
S = 512
D = 1024
KC = D // P
NT = S // P
TW = 256
CH = 64
NCH = S // CH
EPS = 1e-6
NEG = -1e30
INVALID = -3.0e38
TAKEN = -3.4e38
TOPK = 128

F = mybir.dt.float32
R = mybir.dt.float32r
ALU = mybir.AluOpType
ACT = mybir.ActivationFunctionType
AX = mybir.AxisListType.X

STAGES = [("values", 1, 4, 8), ("gates", 2, 2, 4), ("mix1", 4, 4, 8), ("join1", 2, 2, 8), ("out1", 2, 2, 4),
          ("index", 1, 3, 6), ("gla", 2, 3, 6), ("dsa", 2, 3, 6), ("outab", 2, 2, 4),
          ("ffn0", 4, 8, 16), ("stick", 4, 3, 6), ("outc", 2, 2, 4), ("ffn1", 4, 8, 16)]
TILE0, BLOCK0 = {}, {}
_t = _b = 0
for _n, _i, _nt, _nb in STAGES:
    TILE0[_n], BLOCK0[_n] = _t, _b
    _t += _i * _nt
    _b += _i * _nb
N_TILES = _t + _t % 2
PER = {n: (nt, nb) for n, _, nt, nb in STAGES}

(G_NORM, G_FINAL, G_MIX0, G_FFN0, G_MIX1, G_FFN1) = range(0, 48, 8)
CW0, CW1, CW2, CB = 48, 52, 56, 60
GQA, GKA, GGLA, GQC, GKC, BGATE, NPAR = 64, 65, 66, 67, 68, 69, 71

C_ID, C_P, C_GM, C_SB, C_SN, NSMALL = 0, 128, 256, 384, 512, 640

OFF = [0, 128, 384, 768]
CBANK = [0, 0, 1, 2]
COFF = [0, 128, 0, 0]
TOFF = [0, 512, 896, 1152]
TBANK = [0, 1, 2, 2]
TBOFF = [0, 0, 0, 256]


class Step:

    def __init__(self, name, i):
        self.i, (self.nt, self.nb) = i, PER[name]
        self.t0, self.b0 = TILE0[name], BLOCK0[name]
        if isinstance(i, int):
            self.t0, self.b0, self.i = self.t0 + i * self.nt, self.b0 + i * self.nb, None

    def _at(self, base, per):
        return base if self.i is None else self.i * per + base

    def tile(self, k):
        return self._at(self.t0 + k, self.nt)

    def slot(self, k):
        return (self.t0 + k) % 2

    def tile_use(self, k):
        assert self.i is None or self.nt % 2 == 0
        return self._at((self.t0 + k) // 2, self.nt // 2)

    def bank(self, k):
        return (self.b0 + k) % 2

    def block_use(self, k):
        return self._at((self.b0 + k) // 2, self.nb // 2)


class Tally:

    def __init__(self, eng, sem):
        self.eng, self.sem, self.done, self.k, self.i, self.per = eng, sem, 0, 0, None, 0

    def loop(self, i, per):
        self.i, self.per, self.k = i, per, 0

    def end(self, n):
        assert self.k == self.per, (self.k, self.per)
        self.done, self.i, self.k = self.done + n * self.per, None, 0

    def step(self, ins):
        ins.then_inc(self.sem, 1)
        if self.i is None:
            self.done += 1
            self.eng.wait_ge(self.sem, self.done)
        else:
            self.k += 1
            self.eng.wait_ge(self.sem, self.i * self.per + (self.done + self.k))


def build(nc, xT, wst, par_d, wg_d, rb_d, small_d, swap_d, tab_d, out):
    with ExitStack() as ctx:
        def sb(name, shape, dt=F):
            return ctx.enter_context(nc.sbuf_tensor(name, shape, dt))

        def sem(name):
            return ctx.enter_context(nc.semaphore(name))

        raw = [sb(f"raw{s}", [P, KC, TW]) for s in range(2)]
        wh = [sb(f"wh{s}", [P, KC, TW], R) for s in range(2)]
        wl = [sb(f"wl{s}", [P, KC, TW], R) for s in range(2)]
        h = sb("h", [P, KC, S])
        nh = sb("nh", [P, KC, S], R)
        nl = sb("nl", [P, KC, S], R)
        ch = sb("ch", [P, KC, S], R)
        cl = sb("cl", [P, KC, S], R)
        wide = sb("wide", [P, 16, S])
        tmp = sb("tmp", [P, 8, S])
        Sb = sb("Sb", [P, 1280])
        PT = sb("PT", [P, 1280])
        tabs = sb("tabs", [P, 4, S])
        sq = sb("sq", [P, 2, S])
        fb = sb("fb", [P, 2, S])
        extra = sb("extra", [P, 516])
        small = sb("small", [P, NSMALL])
        par = sb("par", [P, NPAR])
        wg = Sb[:, 1024:1280]
        ones = sb("ones", [P, P])
        cols = sb("cols", [P, 32])
        iw = sb("iw", [P, NT, 8])
        top8 = sb("top8", [P, 3, 8])
        ps = {b: ctx.enter_context(nc.psum_tensor(f"ps_{b}", [P, S], F))
              for b in ("G0", "G1", "C0", "C1", "C2", "AV", "ST", "SX")}

        ident = small[:, C_ID:C_ID + P]
        bias = tabs[:].rearrange("p a n -> p (a n)").rearrange("p (h n) -> p h n", h=8)
        nmax, ssum, rsum, eps_c, one_r = cols[:, 0:4], cols[:, 4:8], cols[:, 8:12], cols[:, 12:13], cols[:, 13:14]
        gq_scaled = cols[:, 14:15]
        bfar = cols[:, 16:24]

        loaded = sem("loaded")
        raw_full = [sem(f"raw_full{s}") for s in range(2)]
        w_hi, w_lo = sem("w_hi"), sem("w_lo")
        done = {b: sem(f"done_{b}") for b in ps}
        moved = {b: sem(f"moved_{b}") for b in ps}
        consts_set, dve_set = sem("consts_set"), sem("dve_set")
        pool_step = sem("pool_step")
        dve_step, act_step = sem("dve_step"), sem("act_step")
        tanh_set, v_set = sem("tanh_set"), sem("v_set")
        s_max, s_exp, s_rec, p_ready = sem("s_max"), sem("s_exp"), sem("s_rec"), sem("p_ready")
        cat_lo, y_lo, hid_r, hid_hi, hid_lo = (sem(n) for n in ("cat_lo", "y_lo", "hid_r", "hid_hi", "hid_lo"))
        h_final = sem("h_final")
        sq_ready, sq_used = sem("sq_ready"), sem("sq_used")
        st_x, st_y, st_applied = sem("st_x"), sem("st_y"), sem("st_applied")
        n_f, n_hi, n_lo = sem("n_f"), sem("n_hi"), sem("n_lo")
        tables_in = sem("tables_in")
        rope_x, rope_c, rope_out, x_set = sem("rope_x"), sem("rope_c"), sem("rope_out"), sem("x_set")
        idx_acc = sem("idx_acc")
        g_log, g_scan, g_exp, g_prod, g_silu = (sem(n) for n in ("g_log", "g_scan", "g_exp", "g_prod", "g_silu"))
        sp_log, a_ready = sem("sp_log"), sem("a_ready")
        ob_lo = sem("ob_lo")
        stored = sem("stored")

        def passed(eng, sem_, n):
            eng.wait_ge(sem_, n + 1)

        use, count = {}, {}

        def book(bank, key):
            use[key] = (bank, count.get(bank, 0))
            count[bank] = count.get(bank, 0) + 1

        def book_scores(hd):
            for b in range(3):
                book(f"C{b}", ("score", hd, b))

        def book_turns(hd):
            for b in range(3):
                book(f"C{b}", ("turn", hd, b))

        for hd in range(8):
            book_scores(hd)
            book_turns(hd)
            if hd % 2:
                book("AV", ("av", hd))
        IDX = [(t, hh) for t in (1, 2, 3) for hh in range(8)]
        for r in range(5):
            book("SX", ("perm", r))
        book("SX", ("iw",))
        for p in range(2):
            book("SX", ("gate", p))
            for n in (range(16) if p == 0 else ()):
                book(f"C{n % 3}", ("idx", n))
            book("C0", ("turnk", p))
            if p == 0:
                for n in range(16, 20):
                    book(f"C{n % 3}", ("idx", n))
            book("C1", ("state", p, 0))
            book("C2", ("state", p, 1))
            book("AV", ("state", p, 2))
            book("SX", ("state", p, 3))
            book("C0", ("gatt", p, 0))
            book("C1", ("gatt", p, 1))
            if p == 0:
                for n in range(20, 24):
                    book(f"C{n % 3}", ("idx", n))
            book("AV", ("gout", p, 0))
            book("C2", ("gout", p, 1))

        def book_group(hd, prev, rope, last):
            if prev is not None:
                book_turns(prev)
                book_scores(prev + 1)
                book("AV", ("av", prev))
            if hd is not None:
                if rope:
                    for k in range(2):
                        book("SX", ("perm", rope + k))
            if prev is not None:
                book_turns(prev + 1)
            if hd is not None and rope:
                book("SX", ("perm", rope + 2))
            if prev is not None:
                book("AV", ("av", prev + 1))
            if hd is not None:
                book_scores(hd)
                if rope:
                    book("SX", ("perm", rope + 3))

        book_group(8, None, 5, False)
        book_group(10, 8, 9, False)
        book_group(None, 10, 0, True)
        book_group(12, None, 0, False)
        for hd in (14, 16, 18):
            book_group(hd, hd - 2, 0, False)
        book_group(None, 18, 0, True)

        def settled(eng, key):
            b, n = use[key]
            passed(eng, moved[b], n + 1)

        def stands(eng, st, k):
            passed(eng, moved[f"G{st.bank(k)}"], st.block_use(k) + 1)

        def ready(eng, key):
            b, n = use[key]
            passed(eng, done[b], n + 1)

        def release(ins, key):
            ins.then_inc(moved[use[key][0]], 1)

        def bank_of(key):
            return ps[use[key][0]]

        def state_bank(p, c):
            return ("state", p, c // 4 + 2 * (c % 2)), c // 2 % 2 * 256

        STAT, SQ = {}, {}
        nst = nsq = 0
        for key in ([("norm", 0), ("norm", 1), ("norm", 2)] + [("gla", p, j) for p in range(2) for j in range(2)]
                    + [("qk", n) for n in range(8)] + [("norm", 3), ("norm", 4)]
                    + [("qk", n) for n in range(8, 24)] + [("norm", 5)]):
            STAT[key], SQ[key] = nst, nsq
            nst += 1
            nsq += KC if key[0] == "norm" else 1
        H_BEFORE = [0, 8, 16, 24, 56, 64]
        LO_OF = {0: 0, 2: 1, 3: 2, 4: 3, 5: 4}
        GAIN = [G_NORM, G_FINAL, G_MIX0, G_FFN0, G_MIX1, G_FFN1]

        tabA = (tabs[:, 0, :], tabs[:, 1, :])
        tabI = (tabs[:, 2, :], tabs[:, 3, :])

        def values_of(g):
            n = 3 if g % 2 else 12
            return wide[:, n:n + 2, :].rearrange("p a n -> p (a n)").rearrange("p (t n) -> p t n", t=NT)

        block = ctx.enter_context(nc.Block())

        @block.sync
        def _(sp):
            sp.dma_start(h[:], xT.rearrange("(k p) t -> p k t", p=P)).then_inc(loaded, 16)
            sp.dma_start(par[:], par_d).then_inc(loaded, 16)

            def load(slot, tile):
                sp.dma_start(raw[slot][:].rearrange("p k n -> p (k n)"),
                             wst[tile].rearrange("a p n -> (a p) n") if not isinstance(tile, int)
                             else wst[tile]).then_inc(raw_full[slot], 16)

            load(0, 0)
            load(1, 1)
            sp.dma_start(small[:], small_d).then_inc(loaded, 16)
            sp.dma_start(bias, rb_d.rearrange("h p n -> p h n")).then_inc(loaded, 16)
            far = rb_d[:, P - 1:P, 0:1].rearrange("h a b -> (a b) h").to_broadcast([P, 8])
            with nc.allow_non_contiguous_dma(reason="eight words to each partition"):
                sp.dma_start(bfar, far).then_inc(loaded, 16)
            HALF = TILE0["join1"] // 2

            def pair(i):
                for s in range(2):
                    sp.wait_ge(w_lo, i * 2 + (s - 1))
                    load(s, bass.ds(i * 2 + s, 1))

            with sp.Fori(1, HALF + 1) as i:
                pair(i)
            sp.wait_ge(s_max, 32)
            sp.dma_start(tabs[:], tab_d.rearrange("a p n -> p a n")).then_inc(tables_in, 16)
            passed(sp, done["C2"], 16)
            sp.dma_start(wg[32:48, :], wg_d).then_inc(tables_in, 16)
            GLA_END = (TILE0["dsa"] + 1) // 2
            with sp.Fori(HALF + 1, GLA_END) as i:
                pair(i)
            ready(sp, ("gout", 1, 1))
            sp.dma_start(tabs[:, 0:2, :], tab_d[0:2].rearrange("a p n -> p a n")).then_inc(tables_in, 16)
            sp.dma_start(small[:, C_P:C_P + P], swap_d).then_inc(tables_in, 16)
            with sp.Fori(GLA_END, N_TILES // 2) as i:
                pair(i)
            for k in range(KC):
                stands(sp, Step("ffn1", 3), 8 + k)
                sp.dma_start(out[k * P:(k + 1) * P, :], h[:, k, :]).then_inc(stored, 16)
            sp.wait_ge(stored, 16 * KC)

        @block.tensor
        def _(pe):
            mm = nc.tensor.matmul
            booked = {}

            def take(key):
                b, n = use[key]
                assert booked.get(b, 0) == n, (key, booked.get(b, 0), n)
                booked[b] = n + 1
                passed(pe, moved[b], n)

            def take_block(st, k):
                passed(pe, moved[f"G{st.bank(k)}"], st.block_use(k))
                return ps[f"G{st.bank(k)}"]

            def give_block(ins, st, k):
                ins.then_inc(done[f"G{st.bank(k)}"], 1)

            def need_tile(st, k):
                pe.wait_ge(w_lo, st.tile(k) + 1)

            def three(o, ah, al, bh, bl, first, last):
                mm(o, ah, bh, start=first, stop=False)
                mm(o, ah, bl, start=False, stop=False)
                return mm(o, al, bh, start=False, stop=last)

            def project(st, k, tile, col, xh, xl, chunks=range(KC), xoff=0, each=None, end=False):
                o = take_block(st, k)
                s = st.slot(tile)
                chunks = list(chunks)
                for c in chunks:
                    if each is not None:
                        each(c)
                    last = three(o[:], wh[s][:, c, col:col + P], wl[s][:, c, col:col + P],
                                 xh[:, c - xoff, :], xl[:, c - xoff, :], c == chunks[0], c == chunks[-1])
                give_block(last, st, k)

            def project_v(st, k, tile, half, each=None):
                o = take_block(st, k)
                s = st.slot(tile)
                for a in range(2):
                    t = 2 * half + a
                    for c in range(KC):
                        if each is not None and a == 0:
                            each(c)
                        last = three(o[:, a * TW:(a + 1) * TW], nh[:, c, t * P:(t + 1) * P],
                                     nl[:, c, t * P:(t + 1) * P], wh[s][:, c, :],
                                     wl[s][:, c, :], c == 0, c == KC - 1)
                give_block(last, st, k)

            def norm_stat(n):
                q = SQ[("norm", n)]
                if STAT[("norm", n)]:
                    pe.wait_ge(st_applied, STAT[("norm", n)])
                for c in range(KC):
                    pe.wait_ge(sq_ready, q + c + 1)
                    last = mm(ps["ST"][:], ones[:], sq[:, (q + c) % 2, :], start=c == 0, stop=c == KC - 1)
                    last.then_inc(sq_used, 1)

            def head_stat(key):
                q = SQ[key]
                pe.wait_ge(st_applied, STAT[key])
                pe.wait_ge(sq_ready, q + 1)
                mm(ps["ST"][:], ones[:], sq[:, q % 2, :], start=True, stop=True).then_inc(sq_used, 1)

            def scores(hd, q, k, rows, it=None):
                for b in range(3):
                    if it is None:
                        take(("score", hd, b))
                    else:
                        passed(pe, moved[f"C{b}"], it * 4 + 2 * hd)
                for t in range(NT):
                    w = (t + 1) * P
                    last = mm(ps[f"C{CBANK[t]}"][:, COFF[t]:COFF[t] + w], q[rows, t * P:(t + 1) * P],
                              k[rows, 0:w], start=True, stop=True)
                    if t:
                        last.then_inc(done[f"C{CBANK[t]}"], 1)

            def turns(hd, need, it=None):
                for b in range(3):
                    if it is None:
                        take(("turn", hd, b))
                    else:
                        passed(pe, moved[f"C{b}"], it * 4 + 2 * hd + 1)
                for j in range(NT):
                    for t in range(j, NT):
                        if j == 0:
                            need(t)
                        last = nc.tensor.transpose(
                            ps[f"C{TBANK[j]}"][:, TBOFF[j] + (t - j) * P:TBOFF[j] + (t - j + 1) * P],
                            Sb[:, OFF[t] + j * P:OFF[t] + (j + 1) * P], ident)
                    if j != 2:
                        last.then_inc(done[f"C{TBANK[j]}"], 1)

            def weigh(v, rows, turned):
                for j in range(NT):
                    passed(pe, moved[f"C{TBANK[j]}"], turned(TBANK[j]))
                    last = mm(ps["AV"][rows, j * P:S], v(j), PT[:, TOFF[j]:TOFF[j] + (NT - j) * P],
                              start=j == 0, stop=j == NT - 1)
                return last

            for b in ps:
                pe.sem_inc(done[b], 1)
            pe.wait_ge(loaded, 16 * 5)
            pe.wait_ge(consts_set, 1)
            norm_stat(0)

            st = Step("values", 0)
            for k in range(8):
                if k % 2 == 0:
                    need_tile(st, k // 2)
                if k < 4:
                    project_v(st, k, k // 2, k % 2, each=(lambda c: pe.wait_ge(n_lo, c + 1)) if k == 0 else None)
                else:
                    project(st, k, k // 2, k % 2 * P, nh, nl)

            with pe.Fori(0, 2) as i:
                st = Step("gates", i)
                for k in range(4):
                    if k % 2 == 0:
                        need_tile(st, k // 2)
                    project(st, k, k // 2, k % 2 * P, nh, nl)

            with pe.Fori(0, 4) as i:
                st = Step("mix1", i)
                qs, ks = tmp[:, 0, :], tmp[:, 1, :]

                def block_(k):
                    if k % 2 == 0:
                        need_tile(st, k // 2)
                    project(st, k, k // 2, k % 2 * P, nh, nl)

                def sc(a):
                    stands(pe, st, 0)
                    stands(pe, st, 1)
                    scores(a, qs, ks, slice(64 * a, 64 * a + 64), it=i)

                def tr(a):
                    turns(a, lambda t: pe.wait_ge(p_ready, i * 8 + (4 * a + t + 1)), it=i)

                def av(a):
                    if a == 0:
                        passed(pe, moved["AV"], i)
                        pe.wait_ge(v_set, i * 2 + 2)
                    last = weigh(lambda j: tmp[:, 2, j * P + 64 * a:j * P + 64 * a + 64],
                                 slice(64 * a, 64 * a + 64), lambda b: i * 4 + (2 * a + 2))
                    if a == 1:
                        last.then_inc(done["AV"], 1)

                block_(0)
                block_(1)
                sc(0)
                block_(2)
                block_(3)
                tr(0)
                block_(4)
                av(0)
                sc(1)
                block_(5)
                block_(6)
                tr(1)
                block_(7)
                av(1)
            for b in range(3):
                booked[f"C{b}"] = 16
            booked["AV"] = 4

            pe.wait_ge(cat_lo, 4)
            passed(pe, moved["AV"], 4)
            with pe.Fori(0, 2) as i:
                st = Step("join1", i)
                for t in range(2):
                    need_tile(st, t)
                    for c in range(2):
                        k = 4 * t + 2 * c
                        project(st, k, t, c * P, ch, cl, range(0, 4))
                        project(st, k + 1, t, c * P, ch, cl, range(4, 8))

            def out_projection(name, xh, xl, need, chunks=range(KC)):
                with pe.Fori(0, 2) as i:
                    st = Step(name, i)
                    for t in range(2):
                        need_tile(st, t)
                        for c in range(2):
                            project(st, 2 * t + c, t, c * P, xh, xl, chunks,
                                    each=need if c == t == 0 else None)

            out_projection("out1", nh, nl, lambda c: pe.wait_ge(y_lo, c + 1))
            norm_stat(1)
            norm_stat(2)

            def fed_by(n):
                def each(c):
                    pe.wait_ge(n_lo, 8 * LO_OF[n] + c + 1)
                return each

            def perm(r, x):
                take(("perm", r))
                if r < 5:
                    stands(pe, Step("index", 0), r)
                else:
                    pe.wait_ge(rope_x, r - 4)
                mm(ps["SX"][:], small[:, C_P:C_P + P], x, start=True, stop=True).then_inc(done["SX"], 1)

            st = Step("index", 0)
            for k in range(6):
                if k % 2 == 0:
                    need_tile(st, k // 2)
                project(st, k, k // 2, (k % 2) * P, nh, nl, each=fed_by(2) if k == 0 else None)
                if k:
                    perm(k - 1, tmp[:, 2 + (k - 1) % 2, :])

            def index_score(n):
                t, hh = IDX[n]
                rows = slice(64 * (hh % 2), 64 * (hh % 2) + 64)
                take(("idx", n))
                w = (t + 1) * P
                mm(bank_of(("idx", n))[:, 0:w], wide[rows, hh // 2, t * P:(t + 1) * P], wide[rows, 4, 0:w],
                   start=True, stop=True).then_inc(done[use[("idx", n)][0]], 1)

            eb, qe, qm, km, kd = (wide[:, n, :] for n in range(8, 13))
            vg = wide[:, 13:15, :].rearrange("p a n -> p (a n)").rearrange("p (t n) -> p t n", t=NT)
            states = tabs[:].rearrange("p a n -> p (a n)")
            kdt = Sb[:, 0:S]
            for p in range(2):
                st = Step("gla", p)
                if p == 0:
                    take(("iw",))
                    stands(pe, Step("index", 0), 5)
                    for t in range(NT):
                        last = nc.tensor.transpose(ps["SX"][:, t * 8:t * 8 + 8],
                                                   wide[0:8, 15, t * P:(t + 1) * P], ident[0:8, 0:8])
                    last.then_inc(done["SX"], 1)
                take(("gate", p))
                pe.wait_ge(tables_in, 32)
                stands(pe, Step("index", 0), 5)
                mm(ps["SX"][:], wg[32:48, p * P:(p + 1) * P], wide[32:48, 15, :],
                   start=True, stop=True).then_inc(done["SX"], 1)
                if p == 0:
                    pe.wait_ge(rope_out, 5)
                for k in range(6):
                    if k % 2 == 0:
                        need_tile(st, k // 2)
                    if k in (2, 3):
                        project_v(st, k, k // 2, k % 2)
                    else:
                        project(st, k, k // 2, (k % 2) * P, nh, nl)
                    if k == 4:
                        take(("turnk", p))
                        pe.wait_ge(g_prod, 4 * p + 4)
                        for t in range(NT):
                            last = nc.tensor.transpose(ps["C0"][:, t * P:(t + 1) * P], kd[:, t * P:(t + 1) * P], ident)
                        last.then_inc(done["C0"], 1)
                    if p == 0:
                        for n in range(4 * k, 4 * k + 4):
                            if k < 5:
                                index_score(n)
                    if k == 4:
                        settled(pe, ("turnk", p))
                        stands(pe, st, 2)
                        stands(pe, st, 3)
                        for c in range(NCH - 1):
                            key, col = state_bank(p, c)
                            if c in (0, 1, 4, 5):
                                take(key)
                            rows = slice(64 * (c % 2), 64 * (c % 2) + 64)
                            last = mm(bank_of(key)[:, col:col + 256],
                                      kdt[rows, (c // 2) * P:(c // 2) * P + P], vg[rows, c // 2, :],
                                      start=True, stop=True)
                            if c in (2, 3, 5, 6):
                                last.then_inc(done[use[key][0]], 1)
                        for a in range(2):
                            key = ("gatt", p, a)
                            rows = slice(64 * a, 64 * a + 64)
                            take(key)
                            for t in range(NT):
                                last = mm(bank_of(key)[:, t * P:(t + 1) * P], km[rows, t * P:(t + 1) * P],
                                          qm[rows, t * P:(t + 1) * P], start=True, stop=True)
                            last.then_inc(done[use[key][0]], 1)
                    if p == 0 and k == 5:
                        for n in range(20, 24):
                            index_score(n)
                for a in range(2):
                    key = ("gout", p, a)
                    rows = slice(64 * a, 64 * a + 64)
                    take(key)
                    settled(pe, ("gatt", p, a))
                    settled(pe, ("state", p, 1))
                    o = bank_of(key)
                    for t in range(NT):
                        last = mm(o[:, t * P:(t + 1) * P], vg[:, t, a * P:(a + 1) * P],
                                  PT[:, a * S + t * P:a * S + (t + 1) * P], start=t == 0, stop=False,
                                  skip_group_check=True)
                    for c in range(1, NCH):
                        last = mm(o[:, c * CH:(c + 1) * CH],
                                  states[rows, (c - 1) * 256 + a * P:(c - 1) * 256 + (a + 1) * P],
                                  qe[rows, c * CH:(c + 1) * CH], start=False, stop=c == NCH - 1,
                                  skip_group_check=True)
                    last.then_inc(done[use[key][0]], 1)
                for a in range(2):
                    head_stat(("gla", p, a))

            def attention_group(name, g, hd, prev, rope, qk0, need, set_sem, set_at, each0=None):
                st = Step(name, g)
                before = Step(name, g - 1)
                qkbuf = [wide[:, 8 + n, :] for n in range(4)]
                vbuf = values_of(g - 1)

                def block_(k, tile, col):
                    if k % 2 == 0:
                        need_tile(st, tile)
                    if k < 4:
                        project(st, k, tile, col, nh, nl, each=each0 if k == 0 else None)
                    else:
                        project_v(st, k, tile, k % 2)

                def turn_perm(k):
                    if rope:
                        perm(rope + k, tmp[:, 2 + (rope + k) % 2, :])

                def do_av(x, hh):
                    take(("av", hh))
                    stands(pe, before, 4)
                    stands(pe, before, 5)
                    last = weigh(lambda j: vbuf[:, j, x * P:(x + 1) * P], slice(0, P),
                                 lambda b: use[("turn", hh, b)][1] + 1)
                    last.then_inc(done["AV"], 1)

                if hd is not None:
                    block_(0, 0, 0)
                if prev is not None:
                    turns(prev, need(prev))
                    pe.wait_ge(set_sem, set_at)
                    scores(prev + 1, qkbuf[2], qkbuf[3], slice(0, P))
                if hd is not None:
                    block_(1, 0, P)
                if prev is not None:
                    do_av(0, prev)
                if hd is not None:
                    head_stat(("qk", qk0))
                    block_(2, 1, 0)
                    turn_perm(0)
                    head_stat(("qk", qk0 + 1))
                    block_(3, 1, P)
                    turn_perm(1)
                    head_stat(("qk", qk0 + 2))
                if prev is not None:
                    turns(prev + 1, need(prev + 1))
                if hd is not None:
                    block_(4, 2, 0)
                    turn_perm(2)
                    head_stat(("qk", qk0 + 3))
                if prev is not None:
                    do_av(1, prev + 1)
                if hd is not None:
                    pe.wait_ge(set_sem, set_at + 2)
                    scores(hd, qkbuf[0], qkbuf[1], slice(0, P))
                    block_(5, 2, P)
                    turn_perm(3)

            def softmaxed(x):
                return lambda t: pe.wait_ge(p_ready, 4 * x + t + 1)

            def broken(x):
                return lambda t: pe.wait_ge(a_ready, x - 11)

            pe.wait_ge(tables_in, 64)
            for g in range(2):
                attention_group("dsa", g, 8 + 2 * g, 6 + 2 * g if g else None, 5 + 4 * g, 4 * g,
                                softmaxed, rope_out, 5 + 4 * g)
            attention_group("dsa", 2, None, 10, 0, 0, softmaxed, rope_out, 13)

            def mixed0(c):
                if c < 4:
                    settled(pe, ("av", 8 + c))
                else:
                    pe.wait_ge(ob_lo, c - 3)

            out_projection("outab", ch, cl, mixed0, [4, 5, 6, 7, 0, 1, 2, 3])
            norm_stat(3)

            def mlp(name, n, hid0):
                with pe.Fori(0, 4) as i:
                    st = Step(name, i)
                    for t in range(4):
                        need_tile(st, t)
                        for c in range(2):
                            project(st, 2 * t + c, t, c * P, nh, nl, each=fed_by(n) if t == c == 0 else None)

                    def hidden(c):
                        pe.wait_ge(hid_lo, i * 8 + (hid0 + c + 1))

                    for t in range(4, 8):
                        need_tile(st, t)
                        for c in range(2):
                            project(st, 2 * t + c, t, c * P, ch, cl, each=hidden if (t, c) == (4, 0) else None)

            mlp("ffn0", 3, 0)
            norm_stat(4)
            for g in range(4):
                attention_group("stick", g, 12 + 2 * g, 10 + 2 * g if g else None, 0, 8 + 4 * g,
                                broken, x_set, 4 * g, fed_by(4) if g == 0 else None)
            attention_group("stick", 4, None, 18, 0, 0, broken, x_set, 16)
            out_projection("outc", ch, cl, lambda c: settled(pe, ("av", 12 + c)))
            norm_stat(5)
            mlp("ffn1", 5, 32)

        def norm_input(eng, n, c):
            if n == 2:
                eng.wait_ge(h_final, c + 1)
            elif n:
                name, it, k = {1: ("out1", c // 4, c % 4), 3: ("outab", c // 4, c % 4), 4: ("ffn0", 3, 8 + c),
                               5: ("outc", c // 4, c % 4)}[n]
                stands(eng, Step(name, it), k)

        @block.scalar
        def _(act):
            A = nc.scalar.activation
            chain = Tally(act, act_step)

            def split(st, k, kb=None):
                kb = 2 * k if kb is None else kb
                s = st.slot(k + 1)
                act.wait_ge(raw_full[s], st.tile_use(k + 1) * 16 + 16)
                passed(act, done["G1"], st.block_use(kb))
                A(wh[s][:], raw[s][:], ACT.Copy).then_inc(w_hi, 1)

            def ready_block(st, k):
                passed(act, done[f"G{st.bank(k)}"], st.block_use(k) + 1)
                return ps[f"G{st.bank(k)}"]

            def copy_out(dst, st, k, scale=1.0, src=lambda o: o[:]):
                o = ready_block(st, k)
                A(dst, src(o), ACT.Copy, scale=scale).then_inc(moved[f"G{st.bank(k)}"], 1)

            def square(key, c, src):
                q = SQ[key] + c
                if q >= 2:
                    act.wait_ge(sq_used, q - 1)
                A(sq[:, q % 2, :], src, ACT.Square).then_inc(sq_ready, 1)

            def rsqrt(key):
                act.wait_ge(st_x, STAT[key] + 1)
                chain.step(A(tmp[:, 5, :], tmp[:, 7, :], ACT.Ln))
                chain.step(A(tmp[:, 5, :], tmp[:, 5, :], ACT.Exp, scale=-0.5))
                A(tmp[:, 6, :], tmp[:, 5, :], ACT.Square).then_inc(st_y, 1)

            def norm(n):
                for c in range(KC):
                    norm_input(act, n, c)
                    square(("norm", n), c, h[:, c, :])
                rsqrt(("norm", n))

            def norm_high(n):
                for c in range(KC):
                    k = 8 * LO_OF[n] + c
                    act.wait_ge(n_f, k + 1)
                    A(nh[:, c, :], fb[:, c % 2, :], ACT.Copy).then_inc(n_hi, 1)

            def exp_scores(hh, at):
                for t in range(NT):
                    act.wait_ge(s_max, at(t))
                    w = (t + 1) * P
                    A(Sb[:, OFF[t]:OFF[t] + w], Sb[:, OFF[t]:OFF[t] + w], ACT.Exp, bias=nmax[:, t:t + 1],
                      accum_out=ssum[:, t:t + 1]).then_inc(s_exp, 1)

            def turned_out(at):
                for b, (lo, w) in enumerate(((0, 512), (512, 384), (896, 384))):
                    passed(act, done[f"C{b}"], at(b))
                    A(PT[:, lo:lo + w], ps[f"C{b}"][:, 0:w], ACT.Copy).then_inc(moved[f"C{b}"], 1)

            def functions(table):
                nc.scalar.preload_act_table_set(table)

            LOG, TANH = "natural_log_exp_and_others", "exp_and_others"
            functions(LOG)
            act.wait_ge(loaded, 16 * 5)
            act.wait_ge(raw_full[0], 16)
            A(wh[0][:], raw[0][:], ACT.Copy).then_inc(w_hi, 1)
            act.wait_ge(dve_set, 1)
            norm(0)
            norm_high(0)

            functions(TANH)

            def tanh_half(dst, st, k):
                return A(dst, ready_block(st, k)[:], ACT.Tanh, scale=0.5)

            st = Step("values", 0)
            for k in range(8):
                if k % 2 == 0:
                    split(st, k // 2)
                if k < 4:
                    o = ready_block(st, k)
                    j, half = 8 + k // 2 * 4, k % 2
                    for a in range(2):
                        dst = wide[:, j:j + 4:2, (2 * half + a) * P:(2 * half + a + 1) * P]
                        last = A(dst, o[:, a * TW:(a + 1) * TW].rearrange("p (j n) -> p j n", j=2), ACT.Copy)
                    last.then_inc(moved[f"G{st.bank(k)}"], 1)
                else:
                    tanh_half(tmp[:, 5 + k % 2, :], st, k).then_inc(tanh_set, 1)
            with act.Fori(0, 2) as i:
                st = Step("gates", i)
                for k in range(4):
                    if k % 2 == 0:
                        split(st, k // 2)
                    tanh_half(wide[:, bass.ds(i * 4 + k, 1), :].rearrange("p a n -> p (a n)"), st, k).then_inc(
                        moved[f"G{st.bank(k)}"], 1)
            with act.Fori(0, 4) as i:
                st = Step("mix1", i)

                def gate(k):
                    tanh_half(wide[:, bass.ds(i * 2 + (8 + k - 6), 1), :].rearrange("p a n -> p (a n)"), st, k).then_inc(
                        moved[f"G{st.bank(k)}"], 1)

                split(st, 0)
                copy_out(tmp[:, 0, :], st, 0)
                split(st, 1)
                copy_out(tmp[:, 4, :], st, 2)
                exp_scores(0, lambda q: i * 8 + (q + 1))
                turned_out(lambda b: i * 4 + 2)
                split(st, 2)
                exp_scores(1, lambda q: i * 8 + (q + 5))
                tanh_half(tmp[:, 6, :], st, 5).then_inc(tanh_set, 1)
                split(st, 3)
                gate(6)
                turned_out(lambda b: i * 4 + 4)
                gate(7)

            with act.Fori(0, 2) as i:
                st = Step("join1", i)
                for t in range(2):
                    split(st, t, 4 * t)
            with act.Fori(0, 2) as i:
                st = Step("out1", i)
                for t in range(2):
                    split(st, t)
            functions(LOG)
            norm(1)
            norm(2)
            norm_high(2)

            st = Step("index", 0)
            for k in range(6):
                if k % 2 == 0:
                    split(st, k // 2)
                if k < 5:
                    if k >= 2:
                        act.wait_ge(rope_out, k - 1)
                    copy_out(tmp[:, 2 + k % 2, :], st, k)
                else:
                    copy_out(wide[:, 15, :], st, k)

            def index_relu(n):
                t, _ = IDX[n]
                w = (t + 1) * P
                ready(act, ("idx", n))
                if n >= 2:
                    act.wait_ge(idx_acc, n - 1)
                A(sq[:, n % 2, 0:w], bank_of(("idx", n))[:, 0:w], ACT.Relu, scale=0.125).then_inc(
                    moved[use[("idx", n)][0]], 1)

            eb, qe, qm, km, kd = (wide[:, n, :] for n in range(8, 13))
            vg = wide[:, 13:15, :].rearrange("p a n -> p (a n)").rearrange("p (t n) -> p t n", t=NT)
            for p in range(2):
                st = Step("gla", p)
                if p == 0:
                    act.wait_ge(rope_out, 5)
                ready(act, ("gate", p))
                A(tmp[:, 2, :], ps["SX"][:], ACT.Identity, bias=par[:, BGATE + p:BGATE + p + 1]).then_inc(moved["SX"], 1)
                settled(act, ("gate", p))
                chain.step(A(tmp[:, 3, :], tmp[:, 2, :], ACT.Abs))
                chain.step(A(tmp[:, 3, :], tmp[:, 3, :], ACT.Exp, scale=-1.0))
                A(tmp[:, 3, :], tmp[:, 3, :], ACT.Ln, bias=1.0).then_inc(g_log, 1)
                for k in range(6):
                    if k % 2 == 0:
                        split(st, k // 2)
                    if k == 0:
                        if p:
                            act.wait_ge(g_prod, 4)
                        copy_out(tmp[:, 0, :], st, 0, scale=0.125)
                    elif k == 1:
                        copy_out(tmp[:, 1, :], st, 1)
                        act.wait_ge(g_scan, 3 * p + 1)
                        A(eb, tmp[:, 3, :], ACT.Exp, scale=1 / 16).then_inc(g_exp, 1)
                        act.wait_ge(g_scan, 3 * p + 2)
                        A(qm, tmp[:, 2, :], ACT.Exp, scale=1 / 16).then_inc(g_exp, 1)
                        A(km, tmp[:, 2, :], ACT.Exp, scale=-1 / 16).then_inc(g_exp, 1)
                        act.wait_ge(g_scan, 3 * p + 3)
                        A(kd, tmp[:, 4, :], ACT.Exp, scale=1 / 16).then_inc(g_exp, 1)
                    elif k in (2, 3):
                        copy_out(wide[:, 11 + k, :], st, k)
                    elif k == 4:
                        functions(TANH)
                        o = ready_block(st, k)
                        A(Sb[:, 512:1024], o[:], ACT.Tanh, scale=0.5).then_inc(g_silu, 1)
                        ready(act, ("turnk", p))
                        A(Sb[:, 0:S], ps["C0"][:], ACT.Copy).then_inc(moved["C0"], 1)
                    else:
                        o = ready_block(st, k)
                        A(tmp[:, 4, :], o[:], ACT.Tanh, scale=0.5).then_inc(g_silu, 1)
                    if p == 0:
                        for n in range(4 * k, 4 * k + 4):
                            index_relu(n)
                functions(LOG)
                if p == 0:
                    act.wait_ge(idx_acc, 24)
                for a in range(2):
                    ready(act, ("gout", p, a))
                    square(("gla", p, a), 0, bank_of(("gout", p, a))[:])
                for a in range(2):
                    rsqrt(("gla", p, a))

            def attention_group(name, g, hd, prev, qk0, soft):
                st = Step(name, g)

                def evac_qk(n, k):
                    if qk0 + n >= 2:
                        act.wait_ge(st_applied, STAT[("qk", qk0 + n - 2)] + 1)
                    copy_out(tmp[:, n % 2, :], st, k)
                    stands(act, st, k)
                    square(("qk", qk0 + n), 0, tmp[:, n % 2, :])

                def weights(hh):
                    if soft:
                        exp_scores(hh, lambda t: 4 * hh + t + 1)
                        return
                    for b, (lo, w) in enumerate(((0, 384), (384, 384), (768, 512))):
                        ready(act, ("score", hh, b))
                        last = A(Sb[:, lo:lo + w], ps[f"C{b}"][:, 0:w], ACT.Abs)
                    chain.step(last)
                    chain.step(A(Sb[:], Sb[:], ACT.Exp, scale=-1.0))
                    A(Sb[:], Sb[:], ACT.Ln, bias=1.0).then_inc(sp_log, 1)
                    settled(act, ("score", hh, 2))
                    A(Sb[:], Sb[:], ACT.Exp).then_inc(a_ready, 1)

                def turn(hh):
                    turned_out(lambda b: use[("turn", hh, b)][1] + 1)

                if hd is not None:
                    split(st, 0)
                    evac_qk(0, 0)
                if prev is not None:
                    turn(prev)
                    weights(prev + 1)
                if hd is not None:
                    evac_qk(1, 1)
                    rsqrt(("qk", qk0))
                    split(st, 1)
                    evac_qk(2, 2)
                    rsqrt(("qk", qk0 + 1))
                    evac_qk(3, 3)
                    rsqrt(("qk", qk0 + 2))
                if prev is not None:
                    turn(prev + 1)
                if hd is not None:
                    split(st, 2)
                    copy_out(wide[:, (3 if g % 2 else 12), :], st, 4)
                    rsqrt(("qk", qk0 + 3))
                    weights(hd)
                    copy_out(wide[:, (4 if g % 2 else 13), :], st, 5)

            for g in range(2):
                attention_group("dsa", g, 8 + 2 * g, 6 + 2 * g if g else None, 4 * g, True)
            attention_group("dsa", 2, None, 10, 0, True)

            def splits(name):
                with act.Fori(0, 2) as i:
                    st = Step(name, i)
                    for t in range(2):
                        split(st, t)

            splits("outab")
            norm(3)
            norm_high(3)

            def mlp(name, hid0):
                with act.Fori(0, 4) as i:
                    st = Step(name, i)
                    for t in range(4):
                        split(st, t)
                        for c in range(2):
                            k = 2 * t + c
                            o = ready_block(st, k)
                            A(tmp[:, c, :], o[:], ACT.Relu).then_inc(hid_r, 1)
                            stands(act, st, k)
                            A(ch[:, k, :], tmp[:, 2 + c, :], ACT.Copy).then_inc(hid_hi, 1)
                    for t in range(4, 8):
                        split(st, t)

            mlp("ffn0", 0)
            norm(4)
            norm_high(4)
            for g in range(4):
                attention_group("stick", g, 12 + 2 * g, 10 + 2 * g if g else None, 8 + 4 * g, False)
            attention_group("stick", 4, None, 18, 0, False)
            splits("outc")
            norm(5)
            norm_high(5)
            mlp("ffn1", 32)

        @block.gpsimd
        def _(pool):
            g = nc.gpsimd
            g.memset(ones[:], 1.0).then_inc(consts_set, 1)
            pool.wait_ge(loaded, 16 * 5)
            g.memset(bias[0:64, :, 192:256], NEG).then_inc(consts_set, 1)

            def normalise(rec_at):
                pool.wait_ge(s_rec, rec_at)
                pool.sem_inc(pool_step, 1)
                for t in range(NT):
                    w = (t + 1) * P
                    g.tensor_scalar(Sb[:, OFF[t]:OFF[t] + w], Sb[:, OFF[t]:OFF[t] + w], rsum[:, t:t + 1], 1.0,
                                    ALU.mult, ALU.mult).then_inc(p_ready, 1)

            stands(pool, Step("values", 0), 6)
            stands(pool, Step("values", 0), 7)
            with pool.Fori(0, 4) as i:
                passed(pool, moved["AV"], i)
                for a in range(2):
                    g.tensor_copy(tmp[:, 2 + a, :], wide[:, bass.ds(i * 2 + (8 + a), 1), :].rearrange(
                        "p a n -> p (a n)")).then_inc(v_set, 1)
                normalise(i * 2 + 1)
                normalise(i * 2 + 2)

            def rope_cos(r, cos, dst):
                if r < 5:
                    stands(pool, Step("index", 0), r)
                else:
                    pool.wait_ge(rope_x, r - 4)
                if r >= 2:
                    pool.wait_ge(rope_out, r - 1)
                g.tensor_tensor(dst, tmp[:, 2 + r % 2, :], cos, ALU.mult).then_inc(rope_c, 1)

            pool.wait_ge(tables_in, 32)
            for r in range(5):
                rope_cos(r, tabI[0], tmp[:, r % 2, :])

            eb, qe, qm, km, kd = (wide[:, n, :] for n in range(8, 13))
            for p in range(2):
                st = Step("gla", p)
                stands(pool, st, 0)
                pool.wait_ge(g_exp, 4 * p + 1)
                g.tensor_tensor(qe, tmp[:, 0, :], eb, ALU.mult).then_inc(g_prod, 1)
                pool.wait_ge(g_exp, 4 * p + 2)
                g.tensor_tensor(qm, tmp[:, 0, :], qm, ALU.mult).then_inc(g_prod, 1)
                stands(pool, st, 1)
                pool.wait_ge(g_exp, 4 * p + 3)
                g.tensor_tensor(km, tmp[:, 1, :], km, ALU.mult).then_inc(g_prod, 1)
                pool.wait_ge(g_exp, 4 * p + 4)
                g.tensor_tensor(kd, tmp[:, 1, :], kd, ALU.mult).then_inc(g_prod, 1)

            pool.wait_ge(tables_in, 64)
            for gr in range(3):
                if gr:
                    normalise(8 + 2 * gr)
                if gr < 2:
                    for k in range(4):
                        r = 5 + 4 * gr + k
                        rope_cos(r, tabA[0], wide[:, 14 + r % 2, :])
                    normalise(9 + 2 * gr)

        @block.vector
        def _(dve):
            v = nc.vector
            chain = Tally(dve, dve_step)
            step = chain.step

            def split(st, k, kb=None):
                s = st.slot(k + 1)
                dve.wait_ge(w_hi, st.tile(k + 1) + 1)
                v.tensor_tensor(wl[s][:], raw[s][:], wh[s][:].bitcast(F), ALU.subtract).then_inc(w_lo, 1)

            def ready_block(st, k):
                passed(dve, done[f"G{st.bank(k)}"], st.block_use(k) + 1)
                return ps[f"G{st.bank(k)}"][:]

            def moved_block(ins, st, k):
                ins.then_inc(moved[f"G{st.bank(k)}"], 1)
                stands(dve, st, k)

            def moved_use(ins, key):
                ins.then_inc(moved[use[key][0]], 1)
                settled(dve, key)

            def parts(hi, lo, x, sem_):
                step(v.tensor_copy(hi, x))
                v.tensor_tensor(lo, x, hi.bitcast(F), ALU.subtract).then_inc(sem_, 1)

            stt, ts, tt = v.scalar_tensor_tensor, v.tensor_scalar, v.tensor_tensor

            def rsqrt(key, n):
                dve.wait_ge(sq_used, SQ[key] + (KC if key[0] == "norm" else 1))
                ts(tmp[:, 7, :], ps["ST"][:], 1.0 / n, EPS, ALU.mult, ALU.add).then_inc(st_x, 1)
                dve.wait_ge(st_y, STAT[key] + 1)
                step(stt(out=tmp[:, 6, :], in0=tmp[:, 6, :], scalar=-0.5, in1=tmp[:, 7, :], op0=ALU.mult, op1=ALU.mult))
                step(stt(out=tmp[:, 5, :], in0=tmp[:, 6, :], scalar=1.5, in1=tmp[:, 5, :], op0=ALU.add, op1=ALU.mult))
                return tmp[:, 5, :]

            def norm(n):
                y = rsqrt(("norm", n), D)
                if n == 1:
                    for c in range(KC):
                        stt(out=h[:, c, :], in0=h[:, c, :], scalar=par[:, G_FINAL + c:G_FINAL + c + 1], in1=y,
                            op0=ALU.mult, op1=ALU.mult).then_inc(h_final, 1)
                    dve.wait_ge(h_final, KC)
                else:
                    k0 = 8 * LO_OF[n]

                    def scaled(c):
                        stt(out=fb[:, c % 2, :], in0=h[:, c, :], scalar=par[:, GAIN[n] + c:GAIN[n] + c + 1], in1=y,
                            op0=ALU.mult, op1=ALU.mult).then_inc(n_f, 1)

                    scaled(0)
                    scaled(1)
                    for c in range(KC):
                        dve.wait_ge(n_hi, k0 + c + 1)
                        tt(nl[:, c, :], fb[:, c % 2, :], nh[:, c, :].bitcast(F), ALU.subtract).then_inc(n_lo, 1)
                        if c < KC - 2:
                            dve.wait_ge(n_lo, k0 + c + 1)
                            scaled(c + 2)
                v.tensor_copy(cols[:, 13:14], eps_c).then_inc(st_applied, 1)

            def maxima(at):
                for t in range(NT):
                    v.tensor_reduce(nmax[:, t:t + 1], Sb[:, OFF[t]:OFF[t] + (t + 1) * P], AX, ALU.max,
                                    negate=True).then_inc(s_max, 1)
                dve.wait_ge(s_exp, at)
                v.reciprocal(rsum, ssum).then_inc(s_rec, 1)

            for b in ps:
                dve.sem_inc(moved[b], 1)
            dve.wait_ge(loaded, 16 * 5)
            step(v.memset(eps_c, EPS))
            v.memset(extra[:], 0.0).then_inc(dve_set, 1)
            dve.wait_ge(consts_set, 2)
            dve.wait_ge(dve_set, 1)
            dve.wait_ge(w_hi, 1)
            tt(wl[0][:], raw[0][:], wh[0][:].bitcast(F), ALU.subtract).then_inc(w_lo, 1)
            norm(0)

            st = Step("values", 0)
            for k in range(8):
                if k % 2 == 0:
                    split(st, k // 2)
                if k >= 4:
                    dve.wait_ge(tanh_set, k - 3)
                    moved_block(stt(out=wide[:, 2 * k + 1, :], in0=tmp[:, 5 + k % 2, :], scalar=1.0,
                                    in1=ready_block(st, k), op0=ALU.add, op1=ALU.mult), st, k)
            with dve.Fori(0, 2) as i:
                st = Step("gates", i)
                for t in range(2):
                    split(st, t)
            with dve.Fori(0, 4) as i:
                st = Step("mix1", i)
                chain.loop(i, 8)
                conv, th = tmp[:, 5, :], tmp[:, 6, :]
                up = extra

                def col(base):
                    return par[:, bass.ds(i + base, 1)]

                def dyn(t_, base):
                    return t_[:, bass.ds(i + base, 1), :].rearrange("p a n -> p (a n)")

                def biased(a):
                    n = i * 4 + (2 * a + 1)
                    far = bfar[:, bass.ds(i * 2 + a, 1)]

                    def near(lo, hi):
                        return bias[:, bass.ds(i * 2 + a, 1), lo:hi].rearrange("p a n -> p (a n)")

                    passed(dve, done["C0"], n)
                    stt(out=Sb[:, 0:128], in0=ps["C0"][:, 0:128], scalar=0.125, in1=near(128, 256),
                        op0=ALU.mult, op1=ALU.add)
                    stt(out=Sb[:, 128:384], in0=ps["C0"][:, 128:384], scalar=0.125, in1=near(0, 256),
                        op0=ALU.mult, op1=ALU.add).then_inc(moved["C0"], 1)
                    passed(dve, done["C1"], n)
                    ts(Sb[:, 384:512], ps["C1"][:, 0:128], 0.125, far, ALU.mult, ALU.add)
                    stt(out=Sb[:, 512:768], in0=ps["C1"][:, 128:384], scalar=0.125, in1=near(0, 256),
                        op0=ALU.mult, op1=ALU.add).then_inc(moved["C1"], 1)
                    passed(dve, done["C2"], n)
                    ts(Sb[:, 768:1024], ps["C2"][:, 0:256], 0.125, far, ALU.mult, ALU.add)
                    stt(out=Sb[:, 1024:1280], in0=ps["C2"][:, 256:512], scalar=0.125, in1=near(0, 256),
                        op0=ALU.mult, op1=ALU.add).then_inc(moved["C2"], 1)
                    for b in range(3):
                        passed(dve, moved[f"C{b}"], n)
                    maxima(i * 8 + (4 * a + 4))

                split(st, 0)
                moved_block(v.tensor_copy(tmp[:, 1, :], ready_block(st, 1)), st, 1)
                biased(0)
                split(st, 1)
                o = ready_block(st, 3)
                stands(dve, st, 2)
                moved_block(tt(up[:, 2:2 + S], o, tmp[:, 4, :], ALU.mult), st, 3)
                step(ts(conv, up[:, 2:2 + S], col(CW2), col(CB), ALU.mult, ALU.add))
                step(stt(out=conv, in0=up[:, 1:1 + S], scalar=col(CW1), in1=conv, op0=ALU.mult, op1=ALU.add))
                step(stt(out=conv, in0=up[:, 0:S], scalar=col(CW0), in1=conv, op0=ALU.mult, op1=ALU.add))
                split(st, 2)
                moved_block(tt(conv, ready_block(st, 4), conv, ALU.mult), st, 4)
                biased(1)
                dve.wait_ge(tanh_set, i + 5)
                moved_block(stt(out=fb[:, 0, :], in0=th, scalar=1.0, in1=ready_block(st, 5),
                                op0=ALU.add, op1=ALU.mult), st, 5)
                step(stt(out=fb[:, 1, :], in0=fb[:, 0, :], scalar=0.5, in1=conv, op0=ALU.mult, op1=ALU.mult))
                step(v.tensor_copy(dyn(ch, 4), fb[:, 1, :]))
                tt(dyn(cl, 4), fb[:, 1, :], dyn(ch, 4).bitcast(F), ALU.subtract).then_inc(cat_lo, 1)
                split(st, 3)
                passed(dve, done["AV"], i + 1)
                step(stt(out=fb[:, 0, :], in0=ps["AV"][:], scalar=0.5, in1=tmp[:, 3, :], op0=ALU.mult,
                         op1=ALU.mult))
                step(v.tensor_copy(dyn(ch, 0), fb[:, 0, :]))
                step(tt(dyn(cl, 0), fb[:, 0, :], dyn(ch, 0).bitcast(F), ALU.subtract))
                v.tensor_copy(cols[:, 13:14], eps_c).then_inc(moved["AV"], 1)
            chain.end(4)

            with dve.Fori(0, 2) as i:
                st = Step("join1", i)
                chain.loop(i, 8)
                for t in range(2):
                    split(st, t)
                    for c in range(2):
                        k = 4 * t + 2 * c
                        n = 2 * t + c

                        def at(x, base):
                            return x[:, bass.ds(i * 4 + (n + base), 1), :].rearrange("p a n -> p (a n)")

                        stt(out=fb[:, 0, :], in0=at(wide, 0), scalar=1.0, in1=ready_block(st, k),
                            op0=ALU.add, op1=ALU.mult).then_inc(moved[f"G{st.bank(k)}"], 1)
                        moved_block(stt(out=fb[:, 1, :], in0=at(wide, 8), scalar=1.0, in1=ready_block(st, k + 1),
                                        op0=ALU.add, op1=ALU.mult), st, k + 1)
                        stands(dve, st, k)
                        step(tt(fb[:, 0, :], fb[:, 0, :], fb[:, 1, :], ALU.add))
                        step(ts(at(nh, 0), fb[:, 0, :], 0.5, None, ALU.mult))
                        stt(out=at(nl, 0), in0=fb[:, 0, :], scalar=0.5, in1=at(nh, 0).bitcast(F), op0=ALU.mult,
                            op1=ALU.subtract).then_inc(y_lo, 1)
                        dve.wait_ge(y_lo, i * 4 + (n + 1))
            chain.end(2)

            def residual(name):
                with dve.Fori(0, 2) as i:
                    st = Step(name, i)
                    for t in range(2):
                        split(st, t)
                        for c in range(2):
                            k = 2 * t + c
                            hk = h[:, bass.ds(i * 4 + k, 1), :].rearrange("p a n -> p (a n)")
                            moved_block(tt(hk, hk, ready_block(st, k), ALU.add), st, k)

            residual("out1")
            norm(1)
            norm(2)

            step(v.memset(wide[:, 5, 0:P], 0.0))
            step(v.memset(wide[0:64, 5, 64:P], NEG))
            step(v.memset(extra[:, 0:S], 1.0))
            step(v.memset(extra[:, 0:S:CH], 0.0))
            idx = wide[:, 5:8, :].rearrange("p a n -> p (a n)")[:, 0:1280]

            def rope_add(r, sin, cos_part, dst):
                ready(dve, ("perm", r))
                moved_use(tt(tmp[:, 4, :], ps["SX"][:], sin, ALU.mult), ("perm", r))
                dve.wait_ge(rope_c, r + 1)
                ins = tt(dst, tmp[:, 4, :], cos_part, ALU.add)
                ins.then_inc(rope_out, 1)
                dve.wait_ge(rope_out, r + 1)

            dve.wait_ge(tables_in, 32)
            st = Step("index", 0)
            for k in range(6):
                if k % 2 == 0:
                    split(st, k // 2)
                if k:
                    rope_add(k - 1, tabI[1], tmp[:, (k - 1) % 2, :], wide[:, k - 1, :])
            ready(dve, ("iw",))
            moved_use(ts(iw[:].rearrange("p t n -> p (t n)"), ps["SX"][:, 0:32], 8 ** -0.5, None, ALU.mult), ("iw",))

            def index_add(n):
                t, hh = IDX[n]
                w = (t + 1) * P
                settled(dve, ("idx", n))
                acc = idx[:, OFF[t]:OFF[t] + w]
                wcol = iw[:, t, hh:hh + 1]
                if hh == 0:
                    ins = ts(acc, sq[:, n % 2, 0:w], wcol, None, ALU.mult)
                else:
                    ins = stt(out=acc, in0=sq[:, n % 2, 0:w], scalar=wcol, in1=acc, op0=ALU.mult, op1=ALU.add)
                ins.then_inc(idx_acc, 1)
                dve.wait_ge(idx_acc, n + 1)

            m8 = top8

            def topk_rounds(n):
                for _ in range(n):
                    for t in (1, 2, 3):
                        last = v.max(m8[:, t - 1, :], idx[:, OFF[t]:OFF[t] + (t + 1) * P])
                    step(last)
                    for t in (1, 2, 3):
                        s_ = idx[:, OFF[t]:OFF[t] + (t + 1) * P]
                        last = v.match_replace(s_, m8[:, t - 1, :], s_, TAKEN)
                    step(last)

            states = tabs[:].rearrange("p a n -> p (a n)")
            eb = wide[:, 8, :]
            so = (Sb[:, 512:1024], tmp[:, 4, :])
            for p in range(2):
                st = Step("gla", p)
                cum = tmp[:, 3, :].rearrange("p (c t) -> p c t", t=CH)
                dve.wait_ge(g_log, p + 1)
                step(stt(out=tmp[:, 2, :], in0=tmp[:, 2, :], scalar=0.0, in1=tmp[:, 3, :], op0=ALU.min, op1=ALU.subtract))
                v.tensor_tensor_scan(tmp[:, 3, :], extra[:, 0:S], tmp[:, 2, :], 0.0, ALU.mult, ALU.add).then_inc(g_scan, 1)
                dve.wait_ge(g_scan, 3 * p + 1)
                tt(tmp[:, 2, :].rearrange("p (c t) -> p c t", t=CH), cum,
                   cum[:, :, 31:32].to_broadcast([P, NCH, CH]), ALU.subtract).then_inc(g_scan, 1)
                tt(tmp[:, 4, :].rearrange("p (c t) -> p c t", t=CH), cum[:, :, 63:64].to_broadcast([P, NCH, CH]),
                   cum, ALU.subtract).then_inc(g_scan, 1)
                for k in range(6):
                    if k % 2 == 0:
                        split(st, k // 2)
                    if k >= 4:
                        dve.wait_ge(g_silu, 2 * p + k - 3)
                        moved_block(stt(out=so[k - 4], in0=so[k - 4], scalar=1.0, in1=ready_block(st, k),
                                        op0=ALU.add, op1=ALU.mult), st, k)
                    if k == 4 and p == 0:
                        for n in range(16, 20):
                            index_add(n)
                    if k == 4:
                        for c in range(NCH - 1):
                            key, col = state_bank(p, c)
                            ready(dve, key)
                            inc = bank_of(key)[:, col:col + 256]
                            new = states[:, c * 256:(c + 1) * 256]
                            if c == 0:
                                ins = v.tensor_copy(new, inc)
                            else:
                                ins = stt(out=new, in0=states[:, (c - 1) * 256:c * 256],
                                          scalar=eb[:, c * CH + CH - 1:c * CH + CH], in1=inc, op0=ALU.mult, op1=ALU.add)
                            if c in (2, 3, 5, 6):
                                moved_use(ins, key)
                            else:
                                step(ins)
                        for a in range(2):
                            key = ("gatt", p, a)
                            ready(dve, key)
                            moved_use(tt(PT[:, a * S:(a + 1) * S].rearrange("p (t n) -> p t n", t=NT),
                                         bank_of(key)[:].rearrange("p (t n) -> p t n", t=NT),
                                         small[:, C_GM:C_GM + P].rearrange("p (a n) -> p a n", a=1).to_broadcast([P, NT, P]),
                                         ALU.mult), key)
                    if p == 0 and k != 4:
                        for n in range(4 * k, 4 * k + 4):
                            index_add(n)
                    if p == 0 and k == 5:
                        for t in (1, 2, 3):
                            w = (t + 1) * P
                            step(v.memset(idx[0:64, OFF[t] + w - 64:OFF[t] + w], INVALID))
                    if p == 1:
                        topk_rounds(2)
                for a in range(2):
                    key = ("gout", p, a)
                    y = rsqrt(("gla", p, a), P)
                    moved_use(stt(out=fb[:, 0, :], in0=bank_of(key)[:], scalar=par[:, GGLA:GGLA + 1], in1=y,
                                  op0=ALU.mult, op1=ALU.mult), key)
                    v.tensor_copy(cols[:, 13:14], eps_c).then_inc(st_applied, 1)
                    step(stt(out=fb[:, 1, :], in0=fb[:, 0, :], scalar=0.5, in1=so[a], op0=ALU.mult, op1=ALU.mult))
                    parts(ch[:, 4 + 2 * p + a, :], cl[:, 4 + 2 * p + a, :], fb[:, 1, :], ob_lo)
                    dve.wait_ge(ob_lo, 2 * p + a + 1)

            step(ts(gq_scaled, par[:, GQC:GQC + 1], P ** -0.5, None, ALU.mult))
            suffix = wide[:, 0:3, :].rearrange("p a n -> p (a n)")[:, 0:1280]

            def attention_group(name, g, hd, prev, rope, qk0, soft):
                st = Step(name, g)

                def apply(n):
                    y = rsqrt(("qk", qk0 + n), P)
                    if soft:
                        gain = par[:, GKA:GKA + 1] if n % 2 else par[:, GQA:GQA + 1]
                        dst, sem_ = tmp[:, 2 + (rope + n) % 2, :], rope_x
                    else:
                        gain = par[:, GKC:GKC + 1] if n % 2 else gq_scaled
                        dst, sem_ = wide[:, 8 + n, :], x_set
                    stands(dve, st, n)
                    stt(out=dst, in0=tmp[:, n % 2, :], scalar=gain, in1=y, op0=ALU.mult, op1=ALU.mult).then_inc(sem_, 1)
                    v.tensor_copy(cols[:, 13:14], eps_c).then_inc(st_applied, 1)

                def rotated(n):
                    if soft:
                        r = rope + n
                        rope_add(r, tabA[1], wide[:, 14 + r % 2, :], wide[:, 8 + n, :])

                def weights(hh):
                    if soft:
                        for t in range(NT):
                            key = ("score", hh, CBANK[t])
                            w = (t + 1) * P
                            ready(dve, key)
                            ins = stt(out=Sb[:, OFF[t]:OFF[t] + w], in0=bank_of(key)[:, COFF[t]:COFF[t] + w],
                                      scalar=P ** -0.5, in1=idx[:, OFF[t]:OFF[t] + w], op0=ALU.mult, op1=ALU.add)
                            if t:
                                moved_use(ins, key)
                        maxima(4 * hh + 4)
                        return
                    dve.wait_ge(sp_log, hh - 11)
                    for b, (lo, w) in enumerate(((0, 384), (384, 384), (768, 512))):
                        last = stt(out=Sb[:, lo:lo + w], in0=ps[f"C{b}"][:, 0:w], scalar=0.0, in1=Sb[:, lo:lo + w],
                                   op0=ALU.max, op1=ALU.add)
                    step(last)
                    for t in range(NT):
                        d = slice(OFF[t] + t * P, OFF[t] + (t + 1) * P)
                        last = tt(Sb[:, d], Sb[:, d], small[:, C_SB:C_SB + P], ALU.mult)
                    step(last)
                    for t in range(NT):
                        x = Sb[:, OFF[t]:OFF[t] + (t + 1) * P][:, ::-1]
                        last = v.tensor_tensor_scan(suffix[:, OFF[t]:OFF[t] + (t + 1) * P][:, ::-1],
                                                    extra[:, 0:(t + 1) * P], x, 0.0,
                                                    ALU.mult, ALU.add)
                    step(last)
                    for t in range(NT):
                        d = slice(OFF[t] + t * P, OFF[t] + (t + 1) * P)
                        last = tt(suffix[:, d], suffix[:, d], small[:, C_SN:C_SN + P], ALU.subtract)
                    step(last)
                    for b, (lo, w) in enumerate(((0, 384), (384, 384), (768, 512))):
                        moved_use(tt(Sb[:, lo:lo + w], ps[f"C{b}"][:, 0:w], suffix[:, lo:lo + w], ALU.subtract),
                                  ("score", hh, b))

                def output(hh):
                    key = ("av", hh)
                    c = hh - (8 if soft else 12)
                    ready(dve, key)
                    step(v.tensor_copy(ch[:, c, :], bank_of(key)[:]))
                    tt(cl[:, c, :], bank_of(key)[:], ch[:, c, :].bitcast(F), ALU.subtract).then_inc(moved["AV"], 1)

                extra_rounds = 1 if soft and g == 0 else 0
                if hd is not None:
                    split(st, 0)
                    topk_rounds(extra_rounds)
                if prev is not None:
                    weights(prev + 1)
                    output(prev)
                if hd is not None:
                    apply(0)
                    topk_rounds(extra_rounds)
                    split(st, 1)
                    rotated(0)
                    apply(1)
                    topk_rounds(extra_rounds)
                    rotated(1)
                    apply(2)
                    topk_rounds(extra_rounds)
                    split(st, 2)
                    rotated(2)
                    apply(3)
                if prev is not None:
                    output(prev + 1)
                if hd is not None:
                    if extra_rounds:
                        step(ts(idx[:, P:1280], idx[:, P:1280], -3.2e38, NEG, ALU.is_gt, ALU.mult))
                    weights(hd)
                    rotated(3)

            dve.wait_ge(tables_in, 64)
            for g in range(2):
                attention_group("dsa", g, 8 + 2 * g, 6 + 2 * g if g else None, 5 + 4 * g, 4 * g, True)
            attention_group("dsa", 2, None, 10, 0, 0, True)
            residual("outab")
            norm(3)

            def mlp(name, hid0):
                with dve.Fori(0, 4) as i:
                    st = Step(name, i)
                    for t in range(4):
                        split(st, t)
                        for c in range(2):
                            k = 2 * t + c
                            dve.wait_ge(hid_r, i * 8 + (hid0 + k + 1))
                            v.tensor_tensor(tmp[:, 2 + c, :], tmp[:, c, :], tmp[:, c, :], ALU.mult).then_inc(
                                moved[f"G{st.bank(k)}"], 1)
                            dve.wait_ge(hid_hi, i * 8 + (hid0 + k + 1))
                            tt(cl[:, k, :], tmp[:, 2 + c, :], ch[:, k, :].bitcast(F), ALU.subtract).then_inc(hid_lo, 1)
                            if c:
                                dve.wait_ge(hid_lo, i * 8 + (hid0 + k + 1))
                    for t in range(4, 8):
                        split(st, t)
                        for c in range(2):
                            k = 2 * t + c
                            moved_block(tt(h[:, k - 8, :], h[:, k - 8, :], ready_block(st, k), ALU.add), st, k)

            mlp("ffn0", 0)
            step(v.memset(extra[:, 0:S], 1.0))
            norm(4)
            for g in range(4):
                attention_group("stick", g, 12 + 2 * g, 10 + 2 * g if g else None, 0, 8 + 4 * g, False)
            attention_group("stick", 4, None, 18, 0, 0, False)
            residual("outc")
            norm(5)
            mlp("ffn1", 32)


def tiles(a):
    n = a.shape[1] // TW
    return np.ascontiguousarray(a.reshape(KC, P, n, TW).transpose(2, 1, 0, 3)).reshape(n, P, KC * TW)


def blocks(a, *starts):
    return np.concatenate([a[:, s:s + P] for s in starts], 1)


def weight_stream(x):
    w, parts = x["w_in"][0], []
    Q, K, V, ZA, GB, GC, U, ZC, GA, GG = (512 * n for n in (0, 1, 2, 3, 4, 5, 6, 7, 8, 10))
    parts += [w[:, V:V + 512], w[:, ZA:ZA + 512], w[:, GA:GA + D]]
    for j in range(4):
        o = P * j
        parts.append(blocks(w, Q + o, K + o, GC + o, U + o, GB + o, ZC + o, GG + 2 * o, GG + 2 * o + P))
    parts.append(np.concatenate([x["w_att_out"][0], x["w_conv_out"][0]], 0))
    parts.append(x["w_out"][0])
    w = x["w_in_ab_2"][0]
    QA, KA, VA, IQ = 0, 512, 1024, 1536
    IK, IW, QB, KB, VB, GL, OG = 2048, 2112, 2120, 2376, 2632, 3144, 3160
    z = np.zeros((D, P), w.dtype)
    z[:, 0:8] = w[:, IW:IW + 8]
    z[:, 32:48] = w[:, GL:GL + 16]
    parts += [w[:, IQ:IQ + 512], w[:, IK:IK + 64], w[:, IK:IK + 64], z]
    for p in range(2):
        parts.append(blocks(w, QB + P * p, KB + P * p, VB + 2 * P * p, VB + 2 * P * p + P,
                            OG + 2 * P * p, OG + 2 * P * p + P))

    def heads(w, q, k, v, n):
        for a in range(0, n, 2):
            o = P * a
            parts.append(blocks(w, q + o, k + o, q + o + P, k + o + P, v + o, v + o + P))

    def mlp(up, down):
        for g in range(4):
            parts.append(up[:, g * D:(g + 1) * D])
            parts.append(down[g * D:(g + 1) * D])

    heads(w, QA, KA, VA, 4)
    parts.append(x["w_out_ab_2"][0])
    mlp(x["w_up_2"][0], x["w_down_2"][0])
    heads(x["w_in_c_2"][0], 0, D, 2 * D, 8)
    parts.append(x["w_out_c_2"][0])
    mlp(x["w_up_2"][1], x["w_down_2"][1])
    whole = tiles(np.concatenate(parts, 1))
    assert whole.shape[0] in (N_TILES, N_TILES - 1), whole.shape
    if whole.shape[0] < N_TILES:
        whole = np.concatenate([whole, np.zeros((1,) + whole.shape[1:], whole.dtype)], 0)
    return whole


def parameters(x):
    def c(a):
        return np.asarray(a).reshape(-1, P).T
    cols = [x["norm_g"][0], x["final_norm_g"], x["g_mix_2"][0], x["g_ffn_2"][0], x["g_mix_2"][1], x["g_ffn_2"][1],
            x["conv_w"][0, 0], x["conv_w"][0, 1], x["conv_w"][0, 2], x["conv_b"][0], x["gq_a_2"][0], x["gk_a_2"][0],
            x["g_gla_2"][0], x["gq_c_2"][0], x["gk_c_2"][0], x["b_gate_2"][0]]
    return np.ascontiguousarray(np.concatenate([c(a) for a in cols], 1))


def rotary(head):
    rot = head // 4
    half = rot // 2
    inv = np.power(np.float32(500000.0), -np.arange(half, dtype=np.float32) * np.float32(2.0) / np.float32(rot))
    ang = (np.arange(S, dtype=np.float32)[:, None] * inv.astype(np.float32)[None, :]).T
    cos, sin, swap = np.ones((P, S), np.float32), np.zeros((P, S), np.float32), np.zeros((P, P), np.float32)
    for b in range(0, P, head):
        for j in range(half):
            cos[b + j] = cos[b + half + j] = np.cos(ang[j])
            sin[b + j] = sin[b + half + j] = np.sin(ang[j])
            swap[b + half + j, b + j] = -1.0
            swap[b + j, b + half + j] = 1.0
    return cos, sin, swap


def constants():
    small = np.zeros((P, NSMALL), np.float32)
    ca, sa, pa = rotary(128)
    ci, si, pi = rotary(64)
    i, j = np.arange(P)[:, None], np.arange(P)[None, :]
    small[:, C_ID:C_ID + P] = np.eye(P)
    small[:, C_P:C_P + P] = pi
    small[:, C_GM:C_GM + P] = (i <= j) & (i // CH == j // CH)
    small[:, C_SB:C_SB + P] = j < i
    small[:, C_SN:C_SN + P] = np.where(j < i, 0.0, NEG)
    return small, pa, np.stack([ca, sa, ci, si])


def kernel(**inputs):
    import concourse.bacc as bacc
    from concourse.bass_utils import run_bass_kernel_spmd

    x = {k: np.asarray(a) for k, a in inputs.items()}
    small, swap, tables = constants()
    near = np.minimum(P + np.arange(P)[:, None] - np.arange(2 * P)[None, :], P) + P
    arrays = {
        "xT": np.ascontiguousarray(x["x"][0].T), "wst": weight_stream(x), "par_d": parameters(x),
        "wg_d": np.ascontiguousarray(x["w_gate_up_2"][0]), "rb_d": np.ascontiguousarray(x["rel_bias"][0][:, near]),
        "small_d": small, "swap_d": swap, "tab_d": tables,
    }
    nc = bacc.Bacc("TRN2", target_bir_lowering=False, num_devices=1)
    args = [nc.dram_tensor(n, a.shape, mybir.dt.from_np(a.dtype), kind="ExternalInput").ap()
            for n, a in arrays.items()]
    out = nc.dram_tensor("outT", (D, S), F, kind="ExternalOutput").ap()
    build(nc, *args, out)
    r = run_bass_kernel_spmd(nc, [arrays], core_ids=[0])
    return np.ascontiguousarray(r.results[0]["outT"].T)[None]
```

```python
from contextlib import ExitStack

import numpy as np
import concourse.bass as bass
from concourse import mybir

P = 128
S = 512
D = 1024
KC = D // P
NT = S // P
TW = 256
CH = 64
NCH = S // CH
EPS = 1e-6
NEG = -1e30
INVALID = -3.0e38
TAKEN = -3.4e38
TOPK = 128

F = mybir.dt.float32
R = mybir.dt.float32r
ALU = mybir.AluOpType
ACT = mybir.ActivationFunctionType
AX = mybir.AxisListType.X

STAGES = [("values", 1, 4, 8), ("gates", 2, 2, 4), ("mix1", 4, 4, 8), ("join1", 2, 2, 8), ("out1", 2, 2, 4),
          ("index", 1, 3, 6), ("gla", 2, 3, 6), ("dsa", 2, 3, 6), ("outab", 2, 2, 4),
          ("ffn0", 4, 8, 16), ("stick", 4, 3, 6), ("outc", 2, 2, 4), ("ffn1", 4, 8, 16)]
TILE0, BLOCK0 = {}, {}
_t = _b = 0
for _n, _i, _nt, _nb in STAGES:
    TILE0[_n], BLOCK0[_n] = _t, _b
    _t += _i * _nt
    _b += _i * _nb
N_TILES = _t + _t % 2
PER = {n: (nt, nb) for n, _, nt, nb in STAGES}

(G_NORM, G_FINAL, G_MIX0, G_FFN0, G_MIX1, G_FFN1) = range(0, 48, 8)
CW0, CW1, CW2, CB = 48, 52, 56, 60
GQA, GKA, GGLA, GQC, GKC, BGATE, NPAR = 64, 65, 66, 67, 68, 69, 71

C_ID, C_P, C_GM, NSMALL = 0, 128, 256, 384
C_SN = C_GM

OFF = [0, 128, 384, 768]
CBANK = [0, 0, 1, 2]
COFF = [0, 128, 0, 0]
TOFF = [0, 512, 896, 1152]
TBANK = [0, 1, 2, 2]
TBOFF = [0, 0, 0, 256]


class Step:

    def __init__(self, name, i):
        self.i, (self.nt, self.nb) = i, PER[name]
        self.t0, self.b0 = TILE0[name], BLOCK0[name]
        if isinstance(i, int):
            self.t0, self.b0, self.i = self.t0 + i * self.nt, self.b0 + i * self.nb, None

    def _at(self, base, per):
        return base if self.i is None else self.i * per + base

    def tile(self, k):
        return self._at(self.t0 + k, self.nt)

    def slot(self, k):
        return (self.t0 + k) % 2

    def tile_use(self, k):
        assert self.i is None or self.nt % 2 == 0
        return self._at((self.t0 + k) // 2, self.nt // 2)

    def bank(self, k):
        return (self.b0 + k) % 2

    def block_use(self, k):
        return self._at((self.b0 + k) // 2, self.nb // 2)


class Tally:

    def __init__(self, eng, sem):
        self.eng, self.sem, self.done, self.k, self.i, self.per = eng, sem, 0, 0, None, 0

    def loop(self, i, per):
        self.i, self.per, self.k = i, per, 0

    def end(self, n):
        assert self.k == self.per, (self.k, self.per)
        self.done, self.i, self.k = self.done + n * self.per, None, 0

    def step(self, ins):
        ins.then_inc(self.sem, 1)
        if self.i is None:
            self.done += 1
            self.eng.wait_ge(self.sem, self.done)
        else:
            self.k += 1
            self.eng.wait_ge(self.sem, self.i * self.per + (self.done + self.k))


def build(nc, xT, wst, par_d, wg_d, rb_d, small_d, swap_d, tab_d, out):
    with ExitStack() as ctx:
        def sb(name, shape, dt=F):
            return ctx.enter_context(nc.sbuf_tensor(name, shape, dt))

        def sem(name):
            return ctx.enter_context(nc.semaphore(name))

        raw = [sb(f"raw{s}", [P, KC, TW]) for s in range(2)]
        wh = [sb(f"wh{s}", [P, KC, TW], R) for s in range(2)]
        wl = [sb(f"wl{s}", [P, KC, TW], R) for s in range(2)]
        h = sb("h", [P, KC, S])
        nh = sb("nh", [P, KC, S], R)
        nl = sb("nl", [P, KC, S], R)
        ch = sb("ch", [P, KC, S], R)
        cl = sb("cl", [P, KC, S], R)
        mh, ml, oh, ol = ch, cl, nh, nl
        wide = sb("wide", [P, 16, S])
        tmp = sb("tmp", [P, 8, S])
        Sb = sb("Sb", [P, 1280])
        PT = sb("PT", [P, 1280])
        tabs = sb("tabs", [P, 4, S])
        sq = sb("sq", [P, 2, S])
        fb = sb("fb", [P, 2, S])
        extra = sb("extra", [P, 516])
        small = sb("small", [P, NSMALL])
        par = sb("par", [P, NPAR])
        wg = Sb[:, 1024:1280]
        ones = sb("ones", [P, P])
        ident_r = sb("ident_r", [P, P], R)
        mask_r = sb("mask_r", [P, P], R)
        cols = sb("cols", [P, 32])
        iw = sb("iw", [P, NT, 8])
        top8 = sb("top8", [P, 3, 8])
        ps = {b: ctx.enter_context(nc.psum_tensor(f"ps_{b}", [P, S], F))
              for b in ("G0", "G1", "C0", "C1", "C2", "AV", "ST", "SX")}

        ident = small[:, C_ID:C_ID + P]
        bias = tabs[:].rearrange("p a n -> p (a n)").rearrange("p (h n) -> p h n", h=8)
        nmax, ssum, rsum, eps_c, one_r = cols[:, 0:4], cols[:, 4:8], cols[:, 8:12], cols[:, 12:13], cols[:, 13:14]
        gq_scaled = cols[:, 14:15]
        rt = cols[:, 24:28]
        gain2 = sb("gain2", [P, KC])
        acc = [fb[:, n, :] for n in range(2)]
        far_eps = wide[:, 7, :]
        bfar = cols[:, 16:24]

        loaded, par_in = sem("loaded"), sem("par_in")
        h_in = [sem(f"h_in{k}") for k in range(KC)]
        raw_full = [sem(f"raw_full{s}") for s in range(2)]
        w_hi, w_lo = sem("w_hi"), sem("w_lo")
        done = {b: sem(f"done_{b}") for b in ps}
        moved = {b: sem(f"moved_{b}") for b in ps}
        consts_set, dve_set = sem("consts_set"), sem("dve_set")
        pool_step = sem("pool_step")
        dve_step, act_step = sem("dve_step"), sem("act_step")
        tanh_set, v_set = sem("tanh_set"), sem("v_set")
        s_max, s_exp, s_rec, p_ready = sem("s_max"), sem("s_exp"), sem("s_rec"), sem("p_ready")
        cat_lo, y_lo, hid_sq, hid_hi, hid_lo = (sem(n) for n in ("cat_lo", "y_lo", "hid_sq", "hid_hi", "hid_lo"))
        h_final = sem("h_final")
        sq_ready, sq_added, sq_used, acc_set = (sem(n) for n in ("sq_ready", "sq_added", "sq_used", "acc_set"))
        masks_set = sem("masks_set")
        r_set, carried = sem("r_set"), sem("carried")
        st_x, st_y, st_applied = sem("st_x"), sem("st_y"), sem("st_applied")
        n_f, n_hi, n_lo = sem("n_f"), sem("n_hi"), sem("n_lo")
        tables_in = sem("tables_in")
        rope_x, rope_c, rope_out, x_set = sem("rope_x"), sem("rope_c"), sem("rope_out"), sem("x_set")
        idx_acc = sem("idx_acc")
        g_log, g_scan, g_exp, g_prod, g_silu = (sem(n) for n in ("g_log", "g_scan", "g_exp", "g_prod", "g_silu"))
        sp_log, a_ready = sem("sp_log"), sem("a_ready")
        ob_lo = sem("ob_lo")
        stored = sem("stored")

        def passed(eng, sem_, n):
            eng.wait_ge(sem_, n + 1)

        use, count = {}, {}

        def book(bank, key):
            use[key] = (bank, count.get(bank, 0))
            count[bank] = count.get(bank, 0) + 1

        def book_scores(hd):
            for b in range(3):
                book(f"C{b}", ("score", hd, b))

        def book_turns(hd):
            for b in range(3):
                book(f"C{b}", ("turn", hd, b))

        for hd in range(8):
            book_scores(hd)
            book_turns(hd)
            if hd % 2:
                book("AV", ("av", hd))
        IDX = [(t, hh) for t in (1, 2, 3) for hh in range(8)]
        book("AV", ("sum2",))
        book("AV", ("rt", 2))
        for r in range(5):
            book("SX", ("perm", r))
        book("SX", ("iw",))
        for p in range(2):
            book("SX", ("gate", p))
            for n in (range(16) if p == 0 else ()):
                book(f"C{n % 3}", ("idx", n))
            book("C0", ("turnk", p))
            if p == 0:
                for n in range(16, 20):
                    book(f"C{n % 3}", ("idx", n))
            book("C1", ("state", p, 0))
            book("C2", ("state", p, 1))
            book("AV", ("state", p, 2))
            book("SX", ("state", p, 3))
            book("C0", ("gatt", p, 0))
            book("C1", ("gatt", p, 1))
            if p == 0:
                for n in range(20, 24):
                    book(f"C{n % 3}", ("idx", n))
            book("AV", ("gout", p, 0))
            book("C2", ("gout", p, 1))

        def book_group(prev, rope):
            for hd in (prev, prev + 1) if prev is not None else ():
                book_scores(hd)
                book_turns(hd)
                book("AV", ("av", hd))
            for k in range(4) if rope else ():
                book("SX", ("perm", rope + k))

        for prev, rope in ((None, 5), (8, 9), (10, 0)):
            book_group(prev, rope)
        book("AV", ("rt", 4))
        for prev in (12, 14, 16, 18):
            book_group(prev, 0)

        def settled(eng, key):
            b, n = use[key]
            passed(eng, moved[b], n + 1)

        def stands(eng, st, k):
            passed(eng, moved[f"G{st.bank(k)}"], st.block_use(k) + 1)

        def ready(eng, key):
            b, n = use[key]
            passed(eng, done[b], n + 1)

        def release(ins, key):
            ins.then_inc(moved[use[key][0]], 1)

        def bank_of(key):
            return ps[use[key][0]]

        def state_bank(p, c):
            return ("state", p, c // 4 + 2 * (c % 2)), c // 2 % 2 * 256

        STAT, SQ = {}, {}
        nst = nsq = 0
        for key in ([("norm", 0), ("norm", 2), ("norm", 1)] + [("gla", p, j) for p in range(2) for j in range(2)]
                    + [("qk", n) for n in range(8)] + [("norm", 3), ("norm", 4)]
                    + [("qk", n) for n in range(8, 24)] + [("norm", 5)]):
            STAT[key], SQ[key] = nst, nsq
            nst += 1
            nsq += {("norm", 2): 2 * KC, ("norm", 1): 0}.get(key, KC if key[0] == "norm" else 1)
        LO_OF = {0: 0, 2: 1, 3: 2, 4: 3, 5: 4}
        ADD_OF = {0: 0, 2: 8, 3: 24, 4: 32, 5: 40}
        GAIN = [par[:, b:b + KC] for b in (G_NORM, G_FINAL)] + [gain2] + [par[:, b:b + KC] for b in (G_FFN0, G_MIX1, G_FFN1)]

        tabA = (tabs[:, 0, :], tabs[:, 1, :])
        tabI = (tabs[:, 2, :], tabs[:, 3, :])

        HALVES = (((0, 0, 384), (1, 384, 384)), ((2, 768, 512),))

        def values_of(g):
            n = 3 if g % 2 else 12
            return wide[:, n:n + 2, :].rearrange("p a n -> p (a n)").rearrange("p (t n) -> p t n", t=NT)

        block = ctx.enter_context(nc.Block())

        @block.sync
        def _(sp):
            for k in range(KC):
                sp.dma_start(h[:, k, :], xT[k * P:(k + 1) * P, :]).then_inc(h_in[k], 16)

            def load(slot, tile):
                sp.dma_start(raw[slot][:].rearrange("p k n -> p (k n)"),
                             wst[tile].rearrange("a p n -> (a p) n") if not isinstance(tile, int)
                             else wst[tile]).then_inc(raw_full[slot], 16)

            sp.dma_start(par[:], par_d).then_inc(par_in, 16)
            load(0, 0)
            load(1, 1)
            sp.dma_start(small[:], small_d).then_inc(loaded, 16)
            sp.dma_start(bias, rb_d.rearrange("h p n -> p h n")).then_inc(loaded, 16)
            far = rb_d[:, P - 1:P, 0:1].rearrange("h a b -> (a b) h").to_broadcast([P, 8])
            with nc.allow_non_contiguous_dma(reason="eight words to each partition"):
                sp.dma_start(bfar, far).then_inc(loaded, 16)
            HALF = TILE0["join1"] // 2

            def pair(i):
                for s in range(2):
                    sp.wait_ge(w_lo, i * 2 + (s - 1))
                    load(s, bass.ds(i * 2 + s, 1))

            with sp.Fori(1, HALF + 1) as i:
                pair(i)
            sp.wait_ge(s_max, 32)
            sp.dma_start(tabs[:], tab_d.rearrange("a p n -> p a n")).then_inc(tables_in, 16)
            passed(sp, done["C2"], 16)
            sp.dma_start(wg[32:48, :], wg_d).then_inc(tables_in, 16)
            GLA_END = (TILE0["dsa"] + 1) // 2
            with sp.Fori(HALF + 1, GLA_END) as i:
                pair(i)
            ready(sp, ("gout", 1, 1))
            sp.dma_start(tabs[:, 0:2, :], tab_d[0:2].rearrange("a p n -> p a n")).then_inc(tables_in, 16)
            sp.dma_start(small[:, C_P:C_P + 2 * P], swap_d).then_inc(tables_in, 16)
            with sp.Fori(GLA_END, N_TILES // 2) as i:
                pair(i)
            for k in range(KC):
                stands(sp, Step("ffn1", 3), 8 + k)
                sp.dma_start(out[k * P:(k + 1) * P, :], h[:, k, :]).then_inc(stored, 16)
            sp.wait_ge(stored, 16 * KC)

        @block.tensor
        def _(pe):
            mm = nc.tensor.matmul
            booked = {}

            def take(key):
                b, n = use[key]
                assert booked.get(b, 0) == n, (key, booked.get(b, 0), n)
                booked[b] = n + 1
                passed(pe, moved[b], n)

            def take_block(st, k):
                passed(pe, moved[f"G{st.bank(k)}"], st.block_use(k))
                return ps[f"G{st.bank(k)}"]

            def give_block(ins, st, k):
                ins.then_inc(done[f"G{st.bank(k)}"], 1)

            def need_tile(st, k):
                pe.wait_ge(w_lo, st.tile(k) + 1)

            def three(o, ah, al, bh, bl, first, last):
                mm(o, ah, bh, start=first, stop=False)
                mm(o, ah, bl, start=False, stop=False)
                return mm(o, al, bh, start=False, stop=last)

            def project(st, k, tile, col, xh, xl, chunks=range(KC), xoff=0, each=None, end=False):
                o = take_block(st, k)
                s = st.slot(tile)
                chunks = list(chunks)
                for c in chunks:
                    if each is not None:
                        each(c)
                    last = three(o[:], wh[s][:, c, col:col + P], wl[s][:, c, col:col + P],
                                 xh[:, c - xoff, :], xl[:, c - xoff, :], c == chunks[0], c == chunks[-1])
                give_block(last, st, k)

            def project_some(st, k, xh, xl, chunks, first, last):
                o = take_block(st, k) if first else ps[f"G{st.bank(k)}"]
                s, col = st.slot(k // 2), k % 2 * P
                for c in chunks:
                    ins = three(o[:], wh[s][:, c, col:col + P], wl[s][:, c, col:col + P], xh[:, c, :], xl[:, c, :],
                                first and c == chunks[0], last and c == chunks[-1])
                if last:
                    give_block(ins, st, k)

            def project_v(st, k, tile, half, xh=mh, xl=ml, each=None):
                o = take_block(st, k)
                s = st.slot(tile)
                for a in range(2):
                    t = 2 * half + a
                    for c in range(KC):
                        if each is not None and a == 0:
                            each(c)
                        last = three(o[:, a * TW:(a + 1) * TW], xh[:, c, t * P:(t + 1) * P],
                                     xl[:, c, t * P:(t + 1) * P], wh[s][:, c, :],
                                     wl[s][:, c, :], c == 0, c == KC - 1)
                give_block(last, st, k)

            def norm_stat(n):
                pe.wait_ge(sq_added, ADD_OF[n] + (2 * KC if n == 2 else KC))
                if n == 2:
                    take(("sum2",))
                    mm(ps["AV"][:], ones[:], acc[1], start=True, stop=True).then_inc(done["AV"], 1)
                    pe.sem_inc(sq_used, 1)
                if n:
                    pe.wait_ge(st_applied, STAT[("norm", n)])
                mm(ps["ST"][:], ones[:], acc[0], start=True, stop=True).then_inc(sq_used, 1)

            def token_scales(n, r, at):
                take(("rt", n))
                pe.wait_ge(r_set, at)
                for t in range(NT):
                    last = mm(ps["AV"][:, t:t + 1], r[:, t * P:(t + 1) * P], ident[:, 0:1], start=True, stop=True)
                last.then_inc(done["AV"], 1)

            def head_stat(key):
                q = SQ[key]
                pe.wait_ge(st_applied, STAT[key])
                pe.wait_ge(sq_ready, q + 1)
                mm(ps["ST"][:], ones[:], sq[:, q % 2, :], start=True, stop=True).then_inc(sq_used, 1)

            def scores(hd, q, k, rows, it=None):
                before = it is None and hd >= 12
                for b in range(3):
                    if it is None:
                        take(("score", hd, b))
                    else:
                        passed(pe, moved[f"C{b}"], it * 4 + 2 * hd)
                for t in range(NT):
                    w = (t + 1) * P
                    last = mm(ps[f"C{CBANK[t]}"][:, COFF[t]:COFF[t] + w], q[rows, t * P:(t + 1) * P],
                              k[rows, 0:w], start=True, stop=not before)
                    if before:
                        last = mm(ps[f"C{CBANK[t]}"][:, COFF[t] + t * P:COFF[t] + w], ident_r[:], mask_r[:],
                                  start=False, stop=True)
                    if t:
                        last.then_inc(done[f"C{CBANK[t]}"], 1)

            def turns(hd, need, it=None):
                for b in range(3):
                    if it is None:
                        take(("turn", hd, b))
                    else:
                        passed(pe, moved[f"C{b}"], it * 4 + 2 * hd + 1)
                for j in range(NT):
                    for t in range(j, NT):
                        if j == 0:
                            need(t)
                        last = nc.tensor.transpose(
                            ps[f"C{TBANK[j]}"][:, TBOFF[j] + (t - j) * P:TBOFF[j] + (t - j + 1) * P],
                            Sb[:, OFF[t] + j * P:OFF[t] + (j + 1) * P], ident)
                    if j != 2:
                        last.then_inc(done[f"C{TBANK[j]}"], 1)

            def weigh(v, rows, turned):
                for j in range(NT):
                    passed(pe, moved[f"C{TBANK[j]}"], turned(TBANK[j]))
                    last = mm(ps["AV"][rows, j * P:S], v(j), PT[:, TOFF[j]:TOFF[j] + (NT - j) * P],
                              start=j == 0, stop=j == NT - 1)
                return last

            for b in ps:
                pe.sem_inc(done[b], 1)
            pe.wait_ge(consts_set, 1)
            norm_stat(0)

            st = Step("values", 0)
            for k in range(8):
                if k % 2 == 0:
                    need_tile(st, k // 2)
                if k < 4:
                    project_v(st, k, k // 2, k % 2, nh, nl, each=(lambda c: pe.wait_ge(n_lo, c + 1)) if k == 0 else None)
                else:
                    project(st, k, k // 2, k % 2 * P, nh, nl)

            with pe.Fori(0, 2) as i:
                st = Step("gates", i)
                for k in range(4):
                    if k % 2 == 0:
                        need_tile(st, k // 2)
                    project(st, k, k // 2, k % 2 * P, nh, nl)

            pe.wait_ge(loaded, 16 * 3)
            with pe.Fori(0, 4) as i:
                st = Step("mix1", i)
                qs, ks = tmp[:, 0, :], tmp[:, 1, :]

                def block_(k):
                    if k % 2 == 0:
                        need_tile(st, k // 2)
                    project(st, k, k // 2, k % 2 * P, nh, nl)

                def sc(a):
                    stands(pe, st, 0)
                    stands(pe, st, 1)
                    scores(a, qs, ks, slice(64 * a, 64 * a + 64), it=i)

                def tr(a):
                    turns(a, lambda t: pe.wait_ge(p_ready, i * 8 + (4 * a + t + 1)), it=i)

                def av(a):
                    if a == 0:
                        passed(pe, moved["AV"], i)
                        pe.wait_ge(v_set, i * 2 + 2)
                    last = weigh(lambda j: tmp[:, 2, j * P + 64 * a:j * P + 64 * a + 64],
                                 slice(64 * a, 64 * a + 64), lambda b: i * 4 + (2 * a + 2))
                    if a == 1:
                        last.then_inc(done["AV"], 1)

                block_(0)
                block_(1)
                sc(0)
                block_(2)
                block_(3)
                tr(0)
                block_(4)
                av(0)
                sc(1)
                block_(5)
                block_(6)
                tr(1)
                block_(7)
                av(1)
            for b in range(3):
                booked[f"C{b}"] = 16
            booked["AV"] = 4

            pe.wait_ge(cat_lo, 4)
            passed(pe, moved["AV"], 4)
            with pe.Fori(0, 2) as i:
                st = Step("join1", i)
                for t in range(2):
                    need_tile(st, t)
                    for c in range(2):
                        k = 4 * t + 2 * c
                        project(st, k, t, c * P, ch, cl, range(0, 4))
                        project(st, k + 1, t, c * P, ch, cl, range(4, 8))

            def out_projection(name, xh, xl, need, chunks=range(KC)):
                with pe.Fori(0, 2) as i:
                    st = Step(name, i)
                    for t in range(2):
                        need_tile(st, t)
                        for c in range(2):
                            project(st, 2 * t + c, t, c * P, xh, xl, chunks,
                                    each=need if c == t == 0 else None)

            out_projection("out1", nh, nl, lambda c: pe.wait_ge(y_lo, c + 1))

            def fed_by(n):
                def each(c):
                    if c == KC - 1:
                        norm_stat(n)
                    pe.wait_ge(n_lo, 8 * LO_OF[n] + c + 1)
                return each

            def perm(r, x):
                take(("perm", r))
                if r < 5:
                    stands(pe, Step("index", 0), r)
                else:
                    pe.wait_ge(rope_x, r - 4)
                mm(ps["SX"][:], small[:, C_P:C_P + P], x, start=True, stop=True).then_inc(done["SX"], 1)

            st = Step("index", 0)
            for k in range(6):
                if k % 2 == 0:
                    need_tile(st, k // 2)
                project(st, k, k // 2, (k % 2) * P, mh, ml, each=fed_by(2) if k == 0 else None)
                if k == 1:
                    token_scales(2, fb[:, 1, :], 1)
                if k:
                    perm(k - 1, tmp[:, 2 + (k - 1) % 2, :])

            def index_score(n):
                t, hh = IDX[n]
                rows = slice(64 * (hh % 2), 64 * (hh % 2) + 64)
                take(("idx", n))
                w = (t + 1) * P
                mm(bank_of(("idx", n))[:, 0:w], wide[rows, hh // 2, t * P:(t + 1) * P], wide[rows, 4, 0:w],
                   start=True, stop=True).then_inc(done[use[("idx", n)][0]], 1)

            eb, qe, qm, km, kd = (wide[:, n, :] for n in range(8, 13))
            vg = wide[:, 13:15, :].rearrange("p a n -> p (a n)").rearrange("p (t n) -> p t n", t=NT)
            states = tabs[:].rearrange("p a n -> p (a n)")
            kdt = Sb[:, 0:S]
            for p in range(2):
                st = Step("gla", p)
                if p == 0:
                    take(("iw",))
                    stands(pe, Step("index", 0), 5)
                    for t in range(NT):
                        last = nc.tensor.transpose(ps["SX"][:, t * 8:t * 8 + 8],
                                                   wide[0:8, 15, t * P:(t + 1) * P], ident[0:8, 0:8])
                    last.then_inc(done["SX"], 1)
                take(("gate", p))
                pe.wait_ge(tables_in, 32)
                stands(pe, Step("index", 0), 5)
                mm(ps["SX"][:], wg[32:48, p * P:(p + 1) * P], wide[32:48, 15, :],
                   start=True, stop=True).then_inc(done["SX"], 1)
                if p == 0:
                    pe.wait_ge(rope_out, 5)
                for k in range(6):
                    if k % 2 == 0:
                        need_tile(st, k // 2)
                    if k in (2, 3):
                        project_v(st, k, k // 2, k % 2)
                    else:
                        project(st, k, k // 2, (k % 2) * P, mh, ml)
                    if p and k == 0:
                        head_stat(("gla", 0, 1))
                    if k == 4:
                        take(("turnk", p))
                        pe.wait_ge(g_prod, 4 * p + 4)
                        for t in range(NT):
                            last = nc.tensor.transpose(ps["C0"][:, t * P:(t + 1) * P], kd[:, t * P:(t + 1) * P], ident)
                        last.then_inc(done["C0"], 1)
                    if p == 0:
                        for n in range(4 * k, 4 * k + 4):
                            if k < 5:
                                index_score(n)
                    if k == 4:
                        settled(pe, ("turnk", p))
                        stands(pe, st, 2)
                        stands(pe, st, 3)
                        for c in range(NCH - 1):
                            key, col = state_bank(p, c)
                            if c in (0, 1, 4, 5):
                                take(key)
                            rows = slice(64 * (c % 2), 64 * (c % 2) + 64)
                            last = mm(bank_of(key)[:, col:col + 256],
                                      kdt[rows, (c // 2) * P:(c // 2) * P + P], vg[rows, c // 2, :],
                                      start=True, stop=True)
                            if c in (2, 3, 5, 6):
                                last.then_inc(done[use[key][0]], 1)
                        for a in range(2):
                            key = ("gatt", p, a)
                            rows = slice(64 * a, 64 * a + 64)
                            take(key)
                            for t in range(NT):
                                last = mm(bank_of(key)[:, t * P:(t + 1) * P], km[rows, t * P:(t + 1) * P],
                                          qm[rows, t * P:(t + 1) * P], start=True, stop=True)
                            last.then_inc(done[use[key][0]], 1)
                    if p == 0 and k == 5:
                        for n in range(20, 24):
                            index_score(n)
                for a in range(2):
                    key = ("gout", p, a)
                    rows = slice(64 * a, 64 * a + 64)
                    take(key)
                    settled(pe, ("gatt", p, a))
                    settled(pe, ("state", p, 1))
                    o = bank_of(key)
                    for t in range(NT):
                        last = mm(o[:, t * P:(t + 1) * P], vg[:, t, a * P:(a + 1) * P],
                                  PT[:, a * S + t * P:a * S + (t + 1) * P], start=t == 0, stop=False,
                                  skip_group_check=True)
                    for c in range(1, NCH):
                        last = mm(o[:, c * CH:(c + 1) * CH],
                                  states[rows, (c - 1) * 256 + a * P:(c - 1) * 256 + (a + 1) * P],
                                  qe[rows, c * CH:(c + 1) * CH], start=False, stop=c == NCH - 1,
                                  skip_group_check=True)
                    last.then_inc(done[use[key][0]], 1)
                head_stat(("gla", p, 0))

            def attention_group(name, g, hd, prev, rope, qk0, need, set_sem, set_at, each0=None, ahead=None):
                st = Step(name, g)
                before = Step(name, g - 1)
                qkbuf = [wide[:, 8 + n, :] for n in range(4)]
                vbuf = values_of(g - 1)

                def block_(k, tile, col):
                    if k % 2 == 0:
                        need_tile(st, tile)
                    if k < 4:
                        project(st, k, tile, col, mh, ml, each=each0 if k == 0 else None)
                    else:
                        project_v(st, k, tile, k % 2)

                def turn_perm(k):
                    if rope:
                        perm(rope + k, tmp[:, 2 + (rope + k) % 2, :])

                def do_av(x, hh):
                    take(("av", hh))
                    stands(pe, before, 4)
                    stands(pe, before, 5)
                    last = weigh(lambda j: vbuf[:, j, x * P:(x + 1) * P], slice(0, P),
                                 lambda b: use[("turn", hh, b)][1] + 1)
                    last.then_inc(done["AV"], 1)

                def do_scores(x):
                    pe.wait_ge(set_sem, set_at - 2 + 2 * x)
                    scores(prev + x, qkbuf[2 * x], qkbuf[2 * x + 1], slice(0, P))

                def do_turns(x):
                    turns(prev + x, need(prev + x))

                if prev is not None:
                    do_scores(0)
                if hd is None:
                    so_, standing, mixed = ahead
                    need_tile(so_, 0)
                    for c in standing:
                        mixed(c)
                    project_some(so_, 0, oh, ol, standing, True, False)
                    do_turns(0)
                    project_some(so_, 1, oh, ol, standing, True, False)
                    do_av(0, prev)
                    do_scores(1)
                    c = OUT_CHUNK(prev)
                    mixed(c)
                    project_some(so_, 0, oh, ol, [c], False, False)
                    project_some(so_, 1, oh, ol, [c], False, False)
                    do_turns(1)
                    do_av(1, prev + 1)
                    mixed(c + 1)
                    for k in range(2):
                        project_some(so_, k, oh, ol, [c + 1], False, True)
                    return
                block_(0, 0, 0)
                if name == "dsa" and g == 0:
                    head_stat(("gla", 1, 1))
                block_(1, 0, P)
                if name == "stick" and g == 0:
                    token_scales(4, tmp[:, 5, :], 2)
                head_stat(("qk", qk0))
                if prev is not None:
                    do_turns(0)
                block_(2, 1, 0)
                turn_perm(0)
                head_stat(("qk", qk0 + 1))
                if prev is not None:
                    do_av(0, prev)
                    do_scores(1)
                block_(3, 1, P)
                turn_perm(1)
                head_stat(("qk", qk0 + 2))
                block_(4, 2, 0)
                if rope:
                    head_stat(("qk", qk0 + 3))
                turn_perm(2)
                if prev is not None:
                    do_turns(1)
                block_(5, 2, P)
                if not rope:
                    head_stat(("qk", qk0 + 3))
                turn_perm(3)
                if prev is not None:
                    do_av(1, prev + 1)

            def softmaxed(x):
                return lambda t: pe.wait_ge(p_ready, 4 * x + t + 1)

            def broken(x):
                return lambda t: pe.wait_ge(a_ready, 2 * (x - 12) + (1 if t < 3 else 2))

            def OUT_CHUNK(hd):
                return hd - (8 if hd < 12 else 12)

            def mixed0(c):
                if c < 4:
                    settled(pe, ("av", 8 + c))
                else:
                    pe.wait_ge(ob_lo, c - 3)

            def mixed1(c):
                settled(pe, ("av", 12 + c))

            def rest_of_output(name):
                for k in range(2, 8):
                    st = Step(name, k // 4)
                    if k % 2 == 0:
                        need_tile(st, k % 4 // 2)
                    project(st, k % 4, k % 4 // 2, k % 2 * P, oh, ol)

            pe.wait_ge(tables_in, 64)
            for g in range(2):
                attention_group("dsa", g, 8 + 2 * g, 6 + 2 * g if g else None, 5 + 4 * g, 4 * g,
                                softmaxed, rope_out, 5 + 4 * g)
            attention_group("dsa", 2, None, 10, 0, 0, softmaxed, rope_out, 13,
                            ahead=(Step("outab", 0), [4, 5, 6, 7, 0, 1], mixed0))
            rest_of_output("outab")

            def mlp(name, n, hid0):
                def part(i, first=False):
                    st = Step(name, i)
                    for k in range(8):
                        if k % 2 == 0:
                            need_tile(st, k // 2)
                        project(st, k, k // 2, k % 2 * P, mh, ml, each=fed_by(n) if first and k == 0 else None)

                    def hidden(c):
                        pe.wait_ge(hid_lo, i * 8 + (hid0 + c + 1))

                    for k in range(8, 16):
                        if k % 2 == 0:
                            need_tile(st, k // 2)
                        project(st, k, k // 2, k % 2 * P, oh, ol, each=hidden if k == 8 else None)

                part(0, first=True)
                with pe.Fori(1, 3) as i:
                    part(i)
                part(3)

            mlp("ffn0", 3, 0)
            pe.wait_ge(masks_set, 1)
            for g in range(4):
                attention_group("stick", g, 12 + 2 * g, 10 + 2 * g if g else None, 0, 8 + 4 * g,
                                broken, x_set, 4 * g, fed_by(4) if g == 0 else None)
            attention_group("stick", 4, None, 18, 0, 0, broken, x_set, 16,
                            ahead=(Step("outc", 0), [0, 1, 2, 3, 4, 5], mixed1))
            rest_of_output("outc")
            mlp("ffn1", 5, 32)
        @block.scalar
        def _(act):
            A = nc.scalar.activation
            chain = Tally(act, act_step)

            def split(st, k, kb=None):
                kb = 2 * k if kb is None else kb
                s = st.slot(k + 1)
                act.wait_ge(raw_full[s], st.tile_use(k + 1) * 16 + 16)
                passed(act, done["G1"], st.block_use(kb))
                A(wh[s][:], raw[s][:], ACT.Copy).then_inc(w_hi, 1)

            def ready_block(st, k):
                passed(act, done[f"G{st.bank(k)}"], st.block_use(k) + 1)
                return ps[f"G{st.bank(k)}"]

            def copy_out(dst, st, k, scale=1.0, src=lambda o: o[:]):
                o = ready_block(st, k)
                A(dst, src(o), ACT.Copy, scale=scale).then_inc(moved[f"G{st.bank(k)}"], 1)

            def square(key, src):
                q, m = SQ[key], STAT[key]
                after_norm = [k for k in STAT if STAT[k] == m - 1][0][0] == "norm"
                act.wait_ge(sq_used, m if after_norm else m - 1)
                A(sq[:, q % 2, :], src, ACT.Square).then_inc(sq_ready, 1)

            def rsqrt(key):
                act.wait_ge(st_x, STAT[key] + 1)
                chain.step(A(tmp[:, 5, :], tmp[:, 7, :], ACT.Ln))
                chain.step(A(tmp[:, 5, :], tmp[:, 5, :], ACT.Exp, scale=-0.5))
                A(tmp[:, 6, :], tmp[:, 5, :], ACT.Square).then_inc(st_y, 1)

            def chunk(x, c):
                return x[:, c, :] if isinstance(c, int) else x[:, bass.ds(c, 1), :].rearrange("p a n -> p (a n)")

            def col_at(x, c):
                return x[:, c:c + 1] if isinstance(c, int) else x[:, bass.ds(c, 1)]

            def feed(n, c, odd):
                if not isinstance(c, int):
                    act.sem_inc(carried, 1)
                A(chunk(mh, c), chunk(h, c), ACT.Copy, scale=col_at(GAIN[n], c)).then_inc(n_hi, 1)
                for a in range(2 if n == 2 else 1):
                    j, b = (c * 2 + a, a) if n == 2 else (c, odd)
                    act.wait_ge(sq_added, j + (ADD_OF[n] - 1))
                    if not isinstance(c, int):
                        act.sem_inc(carried, 1)
                    A(sq[:, (SQ[("norm", n)] + b) % 2, :], chunk(h, c), ACT.Square,
                      scale=col_at(GAIN[1], c) if a else 1.0).then_inc(sq_ready, 1)

            def exp_scores(hh, at):
                for t in range(NT):
                    act.wait_ge(s_max, at(t))
                    w = (t + 1) * P
                    A(Sb[:, OFF[t]:OFF[t] + w], Sb[:, OFF[t]:OFF[t] + w], ACT.Exp, bias=nmax[:, t:t + 1],
                      accum_out=ssum[:, t:t + 1]).then_inc(s_exp, 1)

            def turned_out(at):
                for b, (lo, w) in enumerate(((0, 512), (512, 384), (896, 384))):
                    passed(act, done[f"C{b}"], at(b))
                    A(PT[:, lo:lo + w], ps[f"C{b}"][:, 0:w], ACT.Copy).then_inc(moved[f"C{b}"], 1)

            def functions(table):
                nc.scalar.preload_act_table_set(table)

            LOG, TANH = "natural_log_exp_and_others", "exp_and_others"
            functions(LOG)
            for c in range(KC):
                act.wait_ge(h_in[c], 16)
                if c >= 2:
                    act.wait_ge(sq_added, c - 1)
                A(sq[:, c % 2, :], h[:, c, :], ACT.Square).then_inc(sq_ready, 1)
            act.wait_ge(raw_full[0], 16)
            A(wh[0][:], raw[0][:], ACT.Copy).then_inc(w_hi, 1)
            rsqrt(("norm", 0))
            for c in range(KC):
                act.wait_ge(n_f, c + 1)
                A(nh[:, c, :], tmp[:, c % 2, :], ACT.Copy).then_inc(n_hi, 1)

            functions(TANH)

            def tanh_half(dst, st, k):
                return A(dst, ready_block(st, k)[:], ACT.Tanh, scale=0.5)

            st = Step("values", 0)
            for k in range(8):
                if k % 2 == 0:
                    split(st, k // 2)
                if k < 4:
                    o = ready_block(st, k)
                    j, half = 8 + k // 2 * 4, k % 2
                    for a in range(2):
                        dst = wide[:, j:j + 4:2, (2 * half + a) * P:(2 * half + a + 1) * P]
                        last = A(dst, o[:, a * TW:(a + 1) * TW].rearrange("p (j n) -> p j n", j=2), ACT.Copy)
                    last.then_inc(moved[f"G{st.bank(k)}"], 1)
                else:
                    tanh_half(tmp[:, 5 + k % 2, :], st, k).then_inc(tanh_set, 1)
            with act.Fori(0, 2) as i:
                st = Step("gates", i)
                for k in range(4):
                    if k % 2 == 0:
                        split(st, k // 2)
                    tanh_half(wide[:, bass.ds(i * 4 + k, 1), :].rearrange("p a n -> p (a n)"), st, k).then_inc(
                        moved[f"G{st.bank(k)}"], 1)
            with act.Fori(0, 4) as i:
                st = Step("mix1", i)

                def gate(k):
                    tanh_half(wide[:, bass.ds(i * 2 + (8 + k - 6), 1), :].rearrange("p a n -> p (a n)"), st, k).then_inc(
                        moved[f"G{st.bank(k)}"], 1)

                split(st, 0)
                copy_out(tmp[:, 0, :], st, 0)
                split(st, 1)
                copy_out(tmp[:, 4, :], st, 2)
                exp_scores(0, lambda q: i * 8 + (q + 1))
                turned_out(lambda b: i * 4 + 2)
                split(st, 2)
                exp_scores(1, lambda q: i * 8 + (q + 5))
                tanh_half(tmp[:, 6, :], st, 5).then_inc(tanh_set, 1)
                split(st, 3)
                gate(6)
                turned_out(lambda b: i * 4 + 4)
                gate(7)

            with act.Fori(0, 2) as i:
                st = Step("join1", i)
                for t in range(2):
                    split(st, t, 4 * t)
            def out_projection(name, n):
                act.wait_ge(sq_used, STAT[("norm", n)])
                with act.Fori(0, 2) as i:
                    st = Step(name, i)
                    for k in range(4):
                        if k % 2 == 0:
                            split(st, k // 2)
                        stands(act, st, k)
                        feed(n, i * 4 + k, k % 2)

            functions(LOG)
            act.wait_ge(dve_set, 1)
            out_projection("out1", 2)

            st = Step("index", 0)
            split(st, 0)
            rsqrt(("norm", 2))
            rsqrt(("norm", 1))
            split(st, 1)
            split(st, 2)

            def values_out(dst, st, k, half):
                o = ready_block(st, k)
                for a in range(2):
                    t = 2 * half + a
                    last = A(dst[:, a * TW:(a + 1) * TW], o[:, a * TW:(a + 1) * TW], ACT.Copy, scale=rt[:, t:t + 1])
                last.then_inc(moved[f"G{st.bank(k)}"], 1)

            def index_relu(n):
                t, _ = IDX[n]
                w = (t + 1) * P
                ready(act, ("idx", n))
                if n >= 2:
                    act.wait_ge(idx_acc, n - 1)
                A(sq[:, n % 2, 0:w], bank_of(("idx", n))[:, 0:w], ACT.Relu, scale=0.125).then_inc(
                    moved[use[("idx", n)][0]], 1)

            eb, qe, qm, km, kd = (wide[:, n, :] for n in range(8, 13))
            vg = wide[:, 13:15, :].rearrange("p a n -> p (a n)").rearrange("p (t n) -> p t n", t=NT)
            for p in range(2):
                st = Step("gla", p)
                if p == 0:
                    act.wait_ge(rope_out, 5)
                ready(act, ("gate", p))
                A(tmp[:, 2, :], ps["SX"][:], ACT.Identity, bias=par[:, BGATE + p:BGATE + p + 1]).then_inc(moved["SX"], 1)
                settled(act, ("gate", p))
                chain.step(A(tmp[:, 3, :], tmp[:, 2, :], ACT.Abs))
                chain.step(A(tmp[:, 3, :], tmp[:, 3, :], ACT.Exp, scale=-1.0))
                A(tmp[:, 3, :], tmp[:, 3, :], ACT.Ln, bias=1.0).then_inc(g_log, 1)
                for k in range(6):
                    if k % 2 == 0:
                        split(st, k // 2)
                    if k == 1:
                        act.wait_ge(g_scan, 3 * p + 1)
                        A(eb, tmp[:, 3, :], ACT.Exp, scale=1 / 16).then_inc(g_exp, 1)
                        act.wait_ge(g_scan, 3 * p + 2)
                        A(qm, tmp[:, 2, :], ACT.Exp, scale=1 / 16).then_inc(g_exp, 1)
                        A(km, tmp[:, 2, :], ACT.Exp, scale=-1 / 16).then_inc(g_exp, 1)
                        act.wait_ge(g_scan, 3 * p + 3)
                        A(kd, kd, ACT.Exp, scale=1 / 16).then_inc(g_exp, 1)
                        if p:
                            rsqrt(("gla", 0, 1))
                    elif k in (2, 3):
                        values_out(wide[:, 11 + k, :], st, k, k - 2)
                    elif k == 4:
                        functions(TANH)
                        if p:
                            act.wait_ge(st_applied, STAT[("gla", 0, 1)] + 1)
                        stands(act, st, k)
                        A(tmp[:, 5, :], Sb[:, 512:1024], ACT.Tanh, scale=0.5).then_inc(g_silu, 1)
                        ready(act, ("turnk", p))
                        A(Sb[:, 0:S], ps["C0"][:], ACT.Copy).then_inc(moved["C0"], 1)
                    elif k == 5:
                        stands(act, st, k)
                        A(tmp[:, 6, :], tmp[:, 4, :], ACT.Tanh, scale=0.5).then_inc(g_silu, 1)
                    if p == 0:
                        for n in range(4 * k, 4 * k + 4):
                            index_relu(n)
                functions(LOG)
                if p == 0:
                    act.wait_ge(idx_acc, 24)
                for a in range(2):
                    ready(act, ("gout", p, a))
                    square(("gla", p, a), bank_of(("gout", p, a))[:])
                rsqrt(("gla", p, 0))

            def attention_group(name, g, hd, prev, qk0, soft):
                st = Step(name, g)

                def evac_qk(n, k):
                    if qk0 + n >= 2:
                        act.wait_ge(st_applied, STAT[("qk", qk0 + n - 2)] + 1)
                    copy_out(tmp[:, n % 2, :], st, k)
                    stands(act, st, k)
                    square(("qk", qk0 + n), tmp[:, n % 2, :])

                def weights(hh):
                    if soft:
                        exp_scores(hh, lambda t: 4 * hh + t + 1)
                        return
                    for banks in HALVES:
                        for b, lo, w in banks:
                            ready(act, ("score", hh, b))
                            last = A(Sb[:, lo:lo + w], ps[f"C{b}"][:, 0:w], ACT.Abs)
                        x = Sb[:, banks[0][1]:lo + w]
                        chain.step(last)
                        chain.step(A(x, x, ACT.Exp, scale=-1.0))
                        A(x, x, ACT.Ln, bias=1.0).then_inc(sp_log, 1)

                def exponential(hh):
                    if not soft:
                        for banks in HALVES:
                            b, lo, w = banks[-1]
                            settled(act, ("score", hh, b))
                            x = Sb[:, banks[0][1]:lo + w]
                            A(x, x, ACT.Exp).then_inc(a_ready, 1)

                def turn(hh):
                    turned_out(lambda b: use[("turn", hh, b)][1] + 1)

                if hd is None:
                    for x in range(2):
                        weights(prev + x)
                        exponential(prev + x)
                        turn(prev + x)
                    return
                split(st, 0)
                if name == "stick" and g == 0:
                    rsqrt(("norm", 4))
                if soft and g == 0:
                    rsqrt(("gla", 1, 1))
                if prev is not None:
                    weights(prev)
                evac_qk(0, 0)
                evac_qk(1, 1)
                if prev is not None:
                    exponential(prev)
                rsqrt(("qk", qk0))
                if prev is not None:
                    turn(prev)
                split(st, 1)
                if name == "stick" and g == 0:
                    settled(act, ("rt", 4))
                evac_qk(2, 2)
                rsqrt(("qk", qk0 + 1))
                if prev is not None:
                    weights(prev + 1)
                evac_qk(3, 3)
                if soft:
                    rsqrt(("qk", qk0 + 2))
                split(st, 2)
                values_out(wide[:, (3 if g % 2 else 12), :], st, 4, 0)
                if soft:
                    rsqrt(("qk", qk0 + 3))
                if prev is not None:
                    exponential(prev + 1)
                if not soft:
                    rsqrt(("qk", qk0 + 2))
                if prev is not None:
                    turn(prev + 1)
                values_out(wide[:, (4 if g % 2 else 13), :], st, 5, 1)
                if not soft:
                    rsqrt(("qk", qk0 + 3))

            for g in range(2):
                attention_group("dsa", g, 8 + 2 * g, 6 + 2 * g if g else None, 4 * g, True)
            attention_group("dsa", 2, None, 10, 0, True)

            out_projection("outab", 3)

            def mlp(name, hid0, key, n):
                def part(i, first=False, last=False):
                    st = Step(name, i)
                    for k in range(8):
                        if k % 2 == 0:
                            split(st, k // 2)
                        if first and k == 0:
                            rsqrt(key)
                        stands(act, st, k)
                        A(oh[:, k, :], tmp[:, k % 2, :], ACT.Square).then_inc(hid_hi, 1)
                    for k in range(8, 16):
                        if k % 2 == 0:
                            split(st, k // 2)
                        if last:
                            stands(act, st, k)
                            feed(n, k - 8, k % 2)

                part(0, first=True)
                with act.Fori(1, 3) as i:
                    part(i)
                if n:
                    act.wait_ge(sq_used, STAT[("norm", n)])
                part(3, last=n is not None)

            mlp("ffn0", 0, ("norm", 3), 4)
            for g in range(4):
                attention_group("stick", g, 12 + 2 * g, 10 + 2 * g if g else None, 8 + 4 * g, False)
            attention_group("stick", 4, None, 18, 0, False)
            out_projection("outc", 5)
            mlp("ffn1", 32, ("norm", 5), None)

        @block.gpsimd
        def _(pool):
            g = nc.gpsimd
            g.memset(ones[:], 1.0).then_inc(consts_set, 1)

            def add_squares(n, c, odd):
                for a in range(2 if n == 2 else 1):
                    j, b = (c * 2 + a, a) if n == 2 else (c, odd)
                    pool.wait_ge(sq_ready, j + (SQ[("norm", n)] + 1))
                    pool.wait_ge(sq_added, j + (ADD_OF[n] - (1 if n == 2 else 0)))
                    g.tensor_tensor(acc[a], acc[a], sq[:, (SQ[("norm", n)] + b) % 2, :], ALU.add).then_inc(sq_added, 1)

            def clear(n):
                if n:
                    pool.wait_ge(sq_used, STAT[("norm", n)])
                for a in range(2 if n == 2 else 1):
                    g.memset(acc[a], 0.0).then_inc(acc_set, 1)
                pool.wait_ge(acc_set, {0: 1, 2: 3, 3: 4, 4: 5, 5: 6}[n])

            clear(0)
            for c in range(KC):
                if c:
                    pool.wait_ge(sq_added, c)
                pool.wait_ge(sq_ready, c + 1)
                g.tensor_tensor(acc[0], acc[0], sq[:, c % 2, :], ALU.add).then_inc(sq_added, 1)
            pool.wait_ge(loaded, 16 * 3)
            g.memset(bias[0:64, :, 192:256], NEG).then_inc(consts_set, 1)

            def normalise(rec_at):
                pool.wait_ge(s_rec, rec_at)
                pool.sem_inc(pool_step, 1)
                for t in range(NT):
                    w = (t + 1) * P
                    g.tensor_scalar(Sb[:, OFF[t]:OFF[t] + w], Sb[:, OFF[t]:OFF[t] + w], rsum[:, t:t + 1], 1.0,
                                    ALU.mult, ALU.mult).then_inc(p_ready, 1)

            stands(pool, Step("values", 0), 6)
            stands(pool, Step("values", 0), 7)
            with pool.Fori(0, 4) as i:
                passed(pool, moved["AV"], i)
                for a in range(2):
                    g.tensor_copy(tmp[:, 2 + a, :], wide[:, bass.ds(i * 2 + (8 + a), 1), :].rearrange(
                        "p a n -> p (a n)")).then_inc(v_set, 1)
                normalise(i * 2 + 1)
                normalise(i * 2 + 2)

            def rope_cos(r, cos, dst):
                if r < 5:
                    stands(pool, Step("index", 0), r)
                else:
                    pool.wait_ge(rope_x, r - 4)
                if r >= 2:
                    pool.wait_ge(rope_out, r - 1)
                g.tensor_tensor(dst, tmp[:, 2 + r % 2, :], cos, ALU.mult).then_inc(rope_c, 1)

            def out_squares(name, n):
                clear(n)
                with pool.Fori(0, 2) as i:
                    for k in range(4):
                        add_squares(n, i * 4 + k, k % 2)

            pool.wait_ge(y_lo, 8)
            out_squares("out1", 2)

            pool.wait_ge(tables_in, 32)
            for r in range(5):
                rope_cos(r, tabI[0], tmp[:, r % 2, :])

            def split(st, k):
                s = st.slot(k + 1)
                pool.wait_ge(w_hi, st.tile(k + 1) + 1)
                pool.wait_ge(w_lo, st.tile(k + 1))
                g.tensor_tensor(wl[s][:], raw[s][:], wh[s][:].bitcast(F), ALU.subtract).then_inc(w_lo, 1)

            eb, qe, qm, km, kd = (wide[:, n, :] for n in range(8, 13))
            for p in range(2):
                st = Step("gla", p)
                split(st, 0)
                stands(pool, st, 0)
                pool.wait_ge(g_exp, 4 * p + 1)
                g.tensor_tensor(qe, tmp[:, 0, :], eb, ALU.mult).then_inc(g_prod, 1)
                pool.wait_ge(g_exp, 4 * p + 2)
                g.tensor_tensor(qm, tmp[:, 0, :], qm, ALU.mult).then_inc(g_prod, 1)
                stands(pool, st, 1)
                pool.wait_ge(g_exp, 4 * p + 3)
                g.tensor_tensor(km, tmp[:, 1, :], km, ALU.mult).then_inc(g_prod, 1)
                pool.wait_ge(g_exp, 4 * p + 4)
                g.tensor_tensor(kd, tmp[:, 1, :], kd, ALU.mult).then_inc(g_prod, 1)
                split(st, 1)
                split(st, 2)

            pool.wait_ge(tables_in, 64)
            for gr in range(3):
                for x in range(2):
                    if gr < 2 and x == 0:
                        split(Step("dsa", gr), 0)
                    if gr:
                        normalise(7 + 2 * gr + x)
                    for r in (5 + 4 * gr + 2 * x, 6 + 4 * gr + 2 * x) if gr < 2 else ():
                        rope_cos(r, tabA[0], wide[:, 14 + r % 2, :])
                        if r % 4 in (1, 3):
                            split(Step("dsa", gr), r % 4 // 2 + 1)

            out_squares("outab", 3)

            def mlp(name, hid0, n):
                def part(i, last=False):
                    st = Step(name, i)
                    for k in range(8):
                        stands(pool, st, k)
                        g.tensor_tensor(tmp[:, 2 + k % 2, :], tmp[:, k % 2, :], tmp[:, k % 2, :], ALU.mult).then_inc(
                            hid_sq, 1)
                    if last:
                        clear(n)
                        for c in range(KC):
                            add_squares(n, c, c % 2)

                with pool.Fori(0, 3) as i:
                    part(i)
                part(3, last=n is not None)

            mlp("ffn0", 0, 4)
            out_squares("outc", 5)
            mlp("ffn1", 32, None)

        @block.vector
        def _(dve):
            v = nc.vector
            chain = Tally(dve, dve_step)
            step = chain.step

            def split(st, k, kb=None):
                s = st.slot(k + 1)
                dve.wait_ge(w_hi, st.tile(k + 1) + 1)
                v.tensor_tensor(wl[s][:], raw[s][:], wh[s][:].bitcast(F), ALU.subtract).then_inc(w_lo, 1)

            def ready_block(st, k):
                passed(dve, done[f"G{st.bank(k)}"], st.block_use(k) + 1)
                return ps[f"G{st.bank(k)}"][:]

            def moved_block(ins, st, k):
                ins.then_inc(moved[f"G{st.bank(k)}"], 1)
                stands(dve, st, k)

            def moved_use(ins, key):
                ins.then_inc(moved[use[key][0]], 1)
                settled(dve, key)

            def parts(hi, lo, x, sem_):
                step(v.tensor_copy(hi, x))
                v.tensor_tensor(lo, x, hi.bitcast(F), ALU.subtract).then_inc(sem_, 1)

            stt, ts, tt = v.scalar_tensor_tensor, v.tensor_scalar, v.tensor_tensor

            def newton(key, y):
                dve.wait_ge(st_y, STAT[key] + 1)
                step(stt(out=tmp[:, 6, :], in0=tmp[:, 6, :], scalar=-0.5, in1=tmp[:, 7, :], op0=ALU.mult, op1=ALU.mult))
                return stt(out=y, in0=tmp[:, 6, :], scalar=1.5, in1=tmp[:, 5, :], op0=ALU.add, op1=ALU.mult)

            def mean_square(key, n, eps=None):
                dve.wait_ge(sq_used, STAT[key] + 1)
                if eps is None:
                    return ts(tmp[:, 7, :], ps["ST"][:], 1.0 / n, EPS, ALU.mult, ALU.add)
                return stt(out=tmp[:, 7, :], in0=ps["ST"][:], scalar=1.0 / n, in1=eps, op0=ALU.mult, op1=ALU.add)

            def applied():
                v.tensor_copy(cols[:, 13:14], eps_c).then_inc(st_applied, 1)

            def rsqrt(key, n, eps=None):
                mean_square(key, n, eps).then_inc(st_x, 1)
                step(newton(key, tmp[:, 5, :]))
                return tmp[:, 5, :]

            def chunk(x, c):
                return x[:, c, :] if isinstance(c, int) else x[:, bass.ds(c, 1), :].rearrange("p a n -> p (a n)")

            def col_at(x, c):
                return x[:, c:c + 1] if isinstance(c, int) else x[:, bass.ds(c, 1)]

            def low(n, c):
                dve.wait_ge(n_hi, c + (8 * LO_OF[n] + 1))
                stt(out=chunk(ml, c), in0=chunk(h, c), scalar=col_at(GAIN[n], c), in1=chunk(mh, c).bitcast(F),
                    op0=ALU.mult, op1=ALU.subtract).then_inc(n_lo, 1)

            def maxima(at):
                for t in range(NT):
                    v.tensor_reduce(nmax[:, t:t + 1], Sb[:, OFF[t]:OFF[t] + (t + 1) * P], AX, ALU.max,
                                    negate=True).then_inc(s_max, 1)
                dve.wait_ge(s_exp, at)
                v.reciprocal(rsum, ssum).then_inc(s_rec, 1)

            for b in ps:
                dve.sem_inc(moved[b], 1)
            step(v.memset(eps_c, EPS))
            step(v.memset(extra[:], 0.0))
            dve.wait_ge(par_in, 16)
            tt(gain2[:], par[:, G_FINAL:G_FINAL + KC], par[:, G_MIX0:G_MIX0 + KC], ALU.mult).then_inc(dve_set, 1)
            dve.wait_ge(dve_set, 1)
            dve.wait_ge(w_hi, 1)
            tt(wl[0][:], raw[0][:], wh[0][:].bitcast(F), ALU.subtract).then_inc(w_lo, 1)
            y = rsqrt(("norm", 0), D)

            def scaled(c):
                stt(out=tmp[:, c % 2, :], in0=h[:, c, :], scalar=par[:, G_NORM + c:G_NORM + c + 1], in1=y,
                    op0=ALU.mult, op1=ALU.mult).then_inc(n_f, 1)

            scaled(0)
            scaled(1)
            for c in range(KC):
                dve.wait_ge(n_hi, c + 1)
                tt(nl[:, c, :], tmp[:, c % 2, :], nh[:, c, :].bitcast(F), ALU.subtract).then_inc(n_lo, 1)
                if c < KC - 2:
                    dve.wait_ge(n_lo, c + 1)
                    scaled(c + 2)
            applied()
            dve.wait_ge(consts_set, 2)
            dve.wait_ge(loaded, 16 * 3)

            st = Step("values", 0)
            for k in range(8):
                if k % 2 == 0:
                    split(st, k // 2)
                if k >= 4:
                    dve.wait_ge(tanh_set, k - 3)
                    moved_block(stt(out=wide[:, 2 * k + 1, :], in0=tmp[:, 5 + k % 2, :], scalar=1.0,
                                    in1=ready_block(st, k), op0=ALU.add, op1=ALU.mult), st, k)
            with dve.Fori(0, 2) as i:
                st = Step("gates", i)
                for t in range(2):
                    split(st, t)
            with dve.Fori(0, 4) as i:
                st = Step("mix1", i)
                chain.loop(i, 8)
                conv, th = tmp[:, 5, :], tmp[:, 6, :]
                up = extra

                def col(base):
                    return par[:, bass.ds(i + base, 1)]

                def dyn(t_, base):
                    return t_[:, bass.ds(i + base, 1), :].rearrange("p a n -> p (a n)")

                def biased(a):
                    n = i * 4 + (2 * a + 1)
                    far = bfar[:, bass.ds(i * 2 + a, 1)]

                    def near(lo, hi):
                        return bias[:, bass.ds(i * 2 + a, 1), lo:hi].rearrange("p a n -> p (a n)")

                    passed(dve, done["C0"], n)
                    stt(out=Sb[:, 0:128], in0=ps["C0"][:, 0:128], scalar=0.125, in1=near(128, 256),
                        op0=ALU.mult, op1=ALU.add)
                    stt(out=Sb[:, 128:384], in0=ps["C0"][:, 128:384], scalar=0.125, in1=near(0, 256),
                        op0=ALU.mult, op1=ALU.add).then_inc(moved["C0"], 1)
                    passed(dve, done["C1"], n)
                    ts(Sb[:, 384:512], ps["C1"][:, 0:128], 0.125, far, ALU.mult, ALU.add)
                    stt(out=Sb[:, 512:768], in0=ps["C1"][:, 128:384], scalar=0.125, in1=near(0, 256),
                        op0=ALU.mult, op1=ALU.add).then_inc(moved["C1"], 1)
                    passed(dve, done["C2"], n)
                    ts(Sb[:, 768:1024], ps["C2"][:, 0:256], 0.125, far, ALU.mult, ALU.add)
                    stt(out=Sb[:, 1024:1280], in0=ps["C2"][:, 256:512], scalar=0.125, in1=near(0, 256),
                        op0=ALU.mult, op1=ALU.add).then_inc(moved["C2"], 1)
                    for b in range(3):
                        passed(dve, moved[f"C{b}"], n)
                    maxima(i * 8 + (4 * a + 4))

                split(st, 0)
                moved_block(v.tensor_copy(tmp[:, 1, :], ready_block(st, 1)), st, 1)
                biased(0)
                split(st, 1)
                o = ready_block(st, 3)
                stands(dve, st, 2)
                moved_block(tt(up[:, 2:2 + S], o, tmp[:, 4, :], ALU.mult), st, 3)
                step(ts(conv, up[:, 2:2 + S], col(CW2), col(CB), ALU.mult, ALU.add))
                step(stt(out=conv, in0=up[:, 1:1 + S], scalar=col(CW1), in1=conv, op0=ALU.mult, op1=ALU.add))
                step(stt(out=conv, in0=up[:, 0:S], scalar=col(CW0), in1=conv, op0=ALU.mult, op1=ALU.add))
                split(st, 2)
                moved_block(tt(conv, ready_block(st, 4), conv, ALU.mult), st, 4)
                biased(1)
                dve.wait_ge(tanh_set, i + 5)
                moved_block(stt(out=fb[:, 0, :], in0=th, scalar=1.0, in1=ready_block(st, 5),
                                op0=ALU.add, op1=ALU.mult), st, 5)
                step(stt(out=fb[:, 1, :], in0=fb[:, 0, :], scalar=0.5, in1=conv, op0=ALU.mult, op1=ALU.mult))
                step(v.tensor_copy(dyn(ch, 4), fb[:, 1, :]))
                tt(dyn(cl, 4), fb[:, 1, :], dyn(ch, 4).bitcast(F), ALU.subtract).then_inc(cat_lo, 1)
                split(st, 3)
                passed(dve, done["AV"], i + 1)
                step(stt(out=fb[:, 0, :], in0=ps["AV"][:], scalar=0.5, in1=tmp[:, 3, :], op0=ALU.mult,
                         op1=ALU.mult))
                step(v.tensor_copy(dyn(ch, 0), fb[:, 0, :]))
                step(tt(dyn(cl, 0), fb[:, 0, :], dyn(ch, 0).bitcast(F), ALU.subtract))
                dve.sem_inc(moved["AV"], 1)
            chain.end(4)

            with dve.Fori(0, 2) as i:
                st = Step("join1", i)
                chain.loop(i, 8)
                for t in range(2):
                    split(st, t)
                    for c in range(2):
                        k = 4 * t + 2 * c
                        n = 2 * t + c

                        def at(x, base):
                            return x[:, bass.ds(i * 4 + (n + base), 1), :].rearrange("p a n -> p (a n)")

                        stt(out=fb[:, 0, :], in0=at(wide, 0), scalar=1.0, in1=ready_block(st, k),
                            op0=ALU.add, op1=ALU.mult).then_inc(moved[f"G{st.bank(k)}"], 1)
                        moved_block(stt(out=fb[:, 1, :], in0=at(wide, 8), scalar=1.0, in1=ready_block(st, k + 1),
                                        op0=ALU.add, op1=ALU.mult), st, k + 1)
                        stands(dve, st, k)
                        step(tt(fb[:, 0, :], fb[:, 0, :], fb[:, 1, :], ALU.add))
                        step(ts(at(nh, 0), fb[:, 0, :], 0.5, None, ALU.mult))
                        stt(out=at(nl, 0), in0=fb[:, 0, :], scalar=0.5, in1=at(nh, 0).bitcast(F), op0=ALU.mult,
                            op1=ALU.subtract).then_inc(y_lo, 1)
                        dve.wait_ge(y_lo, i * 4 + (n + 1))
            chain.end(2)

            def residual(name, n):
                if name == "outab":
                    dve.wait_ge(w_lo, TILE0["outab"] + 1)
                with dve.Fori(0, 2) as i:
                    st = Step(name, i)
                    for t in range(2):
                        split(st, t)
                        for c in range(2):
                            k = 2 * t + c
                            hk = chunk(h, i * 4 + k)
                            moved_block(tt(hk, hk, ready_block(st, k), ALU.add), st, k)
                            low(n, i * 4 + k)

            residual("out1", 2)

            step(v.memset(wide[:, 5, 0:P], 0.0))
            step(v.memset(wide[0:64, 5, 64:P], NEG))
            step(v.memset(extra[:, 0:S], 1.0))
            step(v.memset(extra[:, 0:S:CH], 0.0))
            idx = wide[:, 5:8, :].rearrange("p a n -> p (a n)")[:, 0:1280]

            def rope_add(r, sin, cos_part, dst):
                ready(dve, ("perm", r))
                moved_use(tt(tmp[:, 4, :], ps["SX"][:], sin, ALU.mult), ("perm", r))
                dve.wait_ge(rope_c, r + 1)
                ins = tt(dst, tmp[:, 4, :], cos_part, ALU.add)
                ins.then_inc(rope_out, 1)
                dve.wait_ge(rope_out, r + 1)

            dve.wait_ge(tables_in, 32)
            st = Step("index", 0)
            r2 = fb[:, 1, :]
            for k in range(6):
                if k % 2 == 0:
                    split(st, k // 2)
                if k == 0:
                    ready(dve, ("sum2",))
                    dve.wait_ge(sq_used, STAT[("norm", 1)] + 1)
                    step(ts(tmp[:, 4, :], ps["ST"][:], EPS / D, EPS * EPS, ALU.mult, ALU.add))
                    stt(out=tmp[:, 7, :], in0=ps["AV"][:], scalar=1.0 / D, in1=tmp[:, 4, :], op0=ALU.mult,
                        op1=ALU.add).then_inc(st_x, 1)
                    newton(("norm", 2), r2).then_inc(r_set, 1)
                    dve.wait_ge(r_set, 1)
                    dve.sem_inc(moved["AV"], 1)
                    dve.sem_inc(st_applied, 1)
                    mean_square(("norm", 1), D).then_inc(st_x, 1)
                dst = tmp[:, 2 + k % 2, :] if k < 5 else wide[:, 15, :]
                moved_block(tt(dst, ready_block(st, k), r2, ALU.mult), st, k)
                if k == 0:
                    step(newton(("norm", 1), tmp[:, 5, :]))
                if k == 1:
                    ready(dve, ("rt", 2))
                    moved_use(v.tensor_copy(rt, ps["AV"][:, 0:4]), ("rt", 2))
                for c in ((), (), (0, 1), (2, 3), (4, 5), (6, 7))[k]:
                    last = stt(out=h[:, c, :], in0=h[:, c, :], scalar=par[:, G_FINAL + c:G_FINAL + c + 1],
                               in1=tmp[:, 5, :], op0=ALU.mult, op1=ALU.mult)
                if k >= 2:
                    step(last)
                if k == 5:
                    applied()
                if k:
                    rope_add(k - 1, tabI[1], tmp[:, (k - 1) % 2, :], wide[:, k - 1, :])
            ready(dve, ("iw",))
            moved_use(ts(iw[:].rearrange("p t n -> p (t n)"), ps["SX"][:, 0:32], 8 ** -0.5, None, ALU.mult), ("iw",))

            def index_add(n):
                t, hh = IDX[n]
                w = (t + 1) * P
                settled(dve, ("idx", n))
                acc = idx[:, OFF[t]:OFF[t] + w]
                wcol = iw[:, t, hh:hh + 1]
                if hh == 0:
                    ins = ts(acc, sq[:, n % 2, 0:w], wcol, None, ALU.mult)
                else:
                    ins = stt(out=acc, in0=sq[:, n % 2, 0:w], scalar=wcol, in1=acc, op0=ALU.mult, op1=ALU.add)
                ins.then_inc(idx_acc, 1)
                dve.wait_ge(idx_acc, n + 1)

            m8 = top8

            def topk_rounds(n):
                for _ in range(n):
                    for t in (1, 2, 3):
                        last = v.max(m8[:, t - 1, :], idx[:, OFF[t]:OFF[t] + (t + 1) * P])
                    step(last)
                    for t in (1, 2, 3):
                        s_ = idx[:, OFF[t]:OFF[t] + (t + 1) * P]
                        last = v.match_replace(s_, m8[:, t - 1, :], s_, TAKEN)
                    step(last)

            states = tabs[:].rearrange("p a n -> p (a n)")
            eb = wide[:, 8, :]
            so = (Sb[:, 512:1024], tmp[:, 4, :])
            def head_out(p, a):
                key = ("gout", p, a)
                y = rsqrt(("gla", p, a), P)
                moved_use(stt(out=fb[:, 0, :], in0=bank_of(key)[:], scalar=par[:, GGLA:GGLA + 1], in1=y,
                              op0=ALU.mult, op1=ALU.mult), key)
                dve.sem_inc(st_applied, 1)
                step(stt(out=fb[:, 0, :], in0=fb[:, 0, :], scalar=0.5, in1=so[a], op0=ALU.mult, op1=ALU.mult))
                parts(oh[:, 4 + 2 * p + a, :], ol[:, 4 + 2 * p + a, :], fb[:, 0, :], ob_lo)
                dve.wait_ge(ob_lo, 2 * p + a + 1)

            for p in range(2):
                st = Step("gla", p)
                cum = tmp[:, 3, :].rearrange("p (c t) -> p c t", t=CH)
                dve.wait_ge(g_log, p + 1)
                step(stt(out=tmp[:, 2, :], in0=tmp[:, 2, :], scalar=0.0, in1=tmp[:, 3, :], op0=ALU.min, op1=ALU.subtract))
                v.tensor_tensor_scan(tmp[:, 3, :], extra[:, 0:S], tmp[:, 2, :], 0.0, ALU.mult, ALU.add).then_inc(g_scan, 1)
                dve.wait_ge(g_scan, 3 * p + 1)
                tt(tmp[:, 2, :].rearrange("p (c t) -> p c t", t=CH), cum,
                   cum[:, :, 31:32].to_broadcast([P, NCH, CH]), ALU.subtract).then_inc(g_scan, 1)
                if p:
                    settled(dve, ("turnk", 0))
                tt(wide[:, 12, :].rearrange("p (c t) -> p c t", t=CH), cum[:, :, 63:64].to_broadcast([P, NCH, CH]),
                   cum, ALU.subtract).then_inc(g_scan, 1)
                for k in range(6):
                    if k < 2:
                        if p:
                            dve.wait_ge(g_prod, 4)
                        moved_block(stt(out=tmp[:, k, :], in0=ready_block(st, k), scalar=(0.125, 1.0)[k], in1=r2,
                                        op0=ALU.mult, op1=ALU.mult), st, k)
                    if p and k == 1:
                        head_out(0, 1)
                    if k >= 4:
                        moved_block(tt(so[k - 4], ready_block(st, k), r2, ALU.mult), st, k)
                        dve.wait_ge(g_silu, 2 * p + k - 3)
                        step(stt(out=so[k - 4], in0=tmp[:, k + 1, :], scalar=1.0, in1=so[k - 4],
                                 op0=ALU.add, op1=ALU.mult))
                    if k == 4 and p == 0:
                        for n in range(16, 20):
                            index_add(n)
                    if k == 4:
                        for c in range(NCH - 1):
                            key, col = state_bank(p, c)
                            ready(dve, key)
                            inc = bank_of(key)[:, col:col + 256]
                            new = states[:, c * 256:(c + 1) * 256]
                            if c == 0:
                                ins = v.tensor_copy(new, inc)
                            else:
                                ins = stt(out=new, in0=states[:, (c - 1) * 256:c * 256],
                                          scalar=eb[:, c * CH + CH - 1:c * CH + CH], in1=inc, op0=ALU.mult, op1=ALU.add)
                            if c in (2, 3, 5, 6):
                                moved_use(ins, key)
                            else:
                                step(ins)
                        for a in range(2):
                            key = ("gatt", p, a)
                            ready(dve, key)
                            moved_use(tt(PT[:, a * S:(a + 1) * S].rearrange("p (t n) -> p t n", t=NT),
                                         bank_of(key)[:].rearrange("p (t n) -> p t n", t=NT),
                                         small[:, C_GM:C_GM + P].rearrange("p (a n) -> p a n", a=1).to_broadcast([P, NT, P]),
                                         ALU.mult), key)
                    if p == 0 and k != 4:
                        for n in range(4 * k, 4 * k + 4):
                            index_add(n)
                    if p == 0 and k == 5:
                        for t in (1, 2, 3):
                            w = (t + 1) * P
                            step(v.memset(idx[0:64, OFF[t] + w - 64:OFF[t] + w], INVALID))
                    if p == 1:
                        topk_rounds((1, 1, 2, 2, 0, 2)[k])
                head_out(p, 0)

            step(ts(gq_scaled, par[:, GQC:GQC + 1], P ** -0.5, None, ALU.mult))
            suffix = wide[:, 0:3, :].rearrange("p a n -> p (a n)")[:, 0:1280]

            def attention_group(name, g, hd, prev, rope, qk0, soft):
                st = Step(name, g)

                def apply(n):
                    y = rsqrt(("qk", qk0 + n), P, wide[:, 0, :] if soft else far_eps)
                    if soft:
                        gain = par[:, GKA:GKA + 1] if n % 2 else par[:, GQA:GQA + 1]
                        dst, sem_ = tmp[:, 2 + (rope + n) % 2, :], rope_x
                    else:
                        gain = par[:, GKC:GKC + 1] if n % 2 else gq_scaled
                        dst, sem_ = wide[:, 8 + n, :], x_set
                    stands(dve, st, n)
                    stt(out=dst, in0=tmp[:, n % 2, :], scalar=gain, in1=y, op0=ALU.mult, op1=ALU.mult).then_inc(sem_, 1)
                    applied()

                def rotated(n):
                    if soft:
                        r = rope + n
                        rope_add(r, tabA[1], wide[:, 14 + r % 2, :], wide[:, 8 + n, :])

                def weights(hh):
                    if soft:
                        for t in range(NT):
                            key = ("score", hh, CBANK[t])
                            w = (t + 1) * P
                            ready(dve, key)
                            ins = stt(out=Sb[:, OFF[t]:OFF[t] + w], in0=bank_of(key)[:, COFF[t]:COFF[t] + w],
                                      scalar=P ** -0.5, in1=idx[:, OFF[t]:OFF[t] + w], op0=ALU.mult, op1=ALU.add)
                            if t:
                                moved_use(ins, key)
                        maxima(4 * hh + 4)
                        return
                    for n, banks in enumerate(HALVES):
                        dve.wait_ge(sp_log, 2 * (hh - 12) + n + 1)
                        for b, lo, w in banks:
                            last = stt(out=Sb[:, lo:lo + w], in0=ps[f"C{b}"][:, 0:w], scalar=0.0,
                                       in1=Sb[:, lo:lo + w], op0=ALU.max, op1=ALU.add)
                        step(last)
                        for t in (3,) if n else (0, 1, 2):
                            back = slice(OFF[t], OFF[t] + (t + 1) * P)
                            last = v.tensor_tensor_scan(suffix[:, back][:, ::-1], extra[:, 0:(t + 1) * P],
                                                        Sb[:, back][:, ::-1], 0.0, ALU.mult, ALU.add)
                        step(last)
                        for b, lo, w in banks:
                            moved_use(tt(Sb[:, lo:lo + w], ps[f"C{b}"][:, 0:w], suffix[:, lo:lo + w], ALU.subtract),
                                      ("score", hh, b))

                def output(hh):
                    key = ("av", hh)
                    c = hh - (8 if soft else 12)
                    ready(dve, key)
                    step(v.tensor_copy(oh[:, c, :], bank_of(key)[:]))
                    tt(ol[:, c, :], bank_of(key)[:], oh[:, c, :].bitcast(F), ALU.subtract).then_inc(moved["AV"], 1)

                if hd is None:
                    for x in range(2):
                        weights(prev + x)
                        output(prev + x)
                    return
                extra_rounds = 1 if soft and g == 0 else 0
                if soft:
                    if g == 0:
                        head_out(1, 1)
                        step(tt(wide[:, 0, :], r2, r2, ALU.mult))
                        step(v.reciprocal(wide[:, 0, :], wide[:, 0, :]))
                        step(ts(wide[:, 0, :], wide[:, 0, :], EPS, None, ALU.mult))
                else:
                    split(st, 0)
                if not soft and g == 0:
                    mean_square(("norm", 4), D).then_inc(st_x, 1)
                    newton(("norm", 4), tmp[:, 5, :]).then_inc(r_set, 1)
                    dve.wait_ge(r_set, 2)
                    step(ts(far_eps, tmp[:, 7, :], EPS, None, ALU.mult))
                    applied()
                    ready(dve, ("rt", 4))
                    moved_use(v.tensor_copy(rt, ps["AV"][:, 0:4]), ("rt", 4))
                if prev is not None:
                    weights(prev)
                apply(0)
                topk_rounds(extra_rounds)
                if not soft:
                    split(st, 1)
                apply(1)
                rotated(0)
                topk_rounds(2 * extra_rounds)
                if prev is not None:
                    output(prev)
                    if not soft:
                        weights(prev + 1)
                rotated(1)
                if soft:
                    if prev is not None:
                        weights(prev + 1)
                    apply(2)
                    topk_rounds(extra_rounds)
                    apply(3)
                    rotated(2)
                    topk_rounds(extra_rounds)
                    rotated(3)
                    topk_rounds(3 * extra_rounds)
                else:
                    split(st, 2)
                    apply(2)
                    apply(3)
                if extra_rounds:
                    step(ts(idx[:, P:1280], idx[:, P:1280], -3.2e38, NEG, ALU.is_gt, ALU.mult))
                if prev is not None:
                    output(prev + 1)

            dve.wait_ge(tables_in, 64)
            step(v.tensor_copy(ident_r[:], ident))
            v.tensor_copy(mask_r[:], small[:, C_SN:C_SN + P]).then_inc(masks_set, 1)
            for g in range(2):
                attention_group("dsa", g, 8 + 2 * g, 6 + 2 * g if g else None, 5 + 4 * g, 4 * g, True)
            attention_group("dsa", 2, None, 10, 0, 0, True)
            residual("outab", 3)

            def mlp(name, hid0, key, n):
                def part(i, first=False, last=False):
                    st = Step(name, i)
                    for k in range(8):
                        if k % 2 == 0:
                            split(st, k // 2)
                        if first and k == 0:
                            rsqrt(key, D)
                        moved_block(stt(out=tmp[:, k % 2, :], in0=ready_block(st, k), scalar=0.0, in1=tmp[:, 5, :],
                                        op0=ALU.max, op1=ALU.mult), st, k)
                        dve.wait_ge(hid_sq, i * 8 + (hid0 + k + 1))
                        dve.wait_ge(hid_hi, i * 8 + (hid0 + k + 1))
                        tt(ol[:, k, :], tmp[:, 2 + k % 2, :], oh[:, k, :].bitcast(F), ALU.subtract).then_inc(hid_lo, 1)
                        dve.wait_ge(hid_lo, i * 8 + (hid0 + k + 1))
                    for k in range(8, 16):
                        if k % 2 == 0:
                            split(st, k // 2)
                        moved_block(tt(h[:, k - 8, :], h[:, k - 8, :], ready_block(st, k), ALU.add), st, k)
                        if last:
                            low(n, k - 8)

                part(0, first=True)
                applied()
                with dve.Fori(1, 3) as i:
                    part(i)
                part(3, last=n is not None)

            mlp("ffn0", 0, ("norm", 3), 4)
            step(v.memset(extra[:, 0:S], 1.0))
            for g in range(4):
                attention_group("stick", g, 12 + 2 * g, 10 + 2 * g if g else None, 0, 8 + 4 * g, False)
            attention_group("stick", 4, None, 18, 0, 0, False)
            residual("outc", 5)
            mlp("ffn1", 32, ("norm", 5), None)


def tiles(a):
    n = a.shape[1] // TW
    return np.ascontiguousarray(a.reshape(KC, P, n, TW).transpose(2, 1, 0, 3)).reshape(n, P, KC * TW)


def blocks(a, *starts):
    return np.concatenate([a[:, s:s + P] for s in starts], 1)


def weight_stream(x):
    w, parts = x["w_in"][0], []
    Q, K, V, ZA, GB, GC, U, ZC, GA, GG = (512 * n for n in (0, 1, 2, 3, 4, 5, 6, 7, 8, 10))
    parts += [w[:, V:V + 512], w[:, ZA:ZA + 512], w[:, GA:GA + D]]
    for j in range(4):
        o = P * j
        parts.append(blocks(w, Q + o, K + o, GC + o, U + o, GB + o, ZC + o, GG + 2 * o, GG + 2 * o + P))
    parts.append(np.concatenate([x["w_att_out"][0], x["w_conv_out"][0]], 0))
    parts.append(x["w_out"][0])
    w = x["w_in_ab_2"][0]
    QA, KA, VA, IQ = 0, 512, 1024, 1536
    IK, IW, QB, KB, VB, GL, OG = 2048, 2112, 2120, 2376, 2632, 3144, 3160
    z = np.zeros((D, P), w.dtype)
    z[:, 0:8] = w[:, IW:IW + 8]
    z[:, 32:48] = w[:, GL:GL + 16]
    parts += [w[:, IQ:IQ + 512], w[:, IK:IK + 64], w[:, IK:IK + 64], z]
    for p in range(2):
        parts.append(blocks(w, QB + P * p, KB + P * p, VB + 2 * P * p, VB + 2 * P * p + P,
                            OG + 2 * P * p, OG + 2 * P * p + P))

    def heads(w, q, k, v, n):
        for a in range(0, n, 2):
            o = P * a
            parts.append(blocks(w, q + o, k + o, q + o + P, k + o + P, v + o, v + o + P))

    def mlp(up, down):
        for g in range(4):
            parts.append(up[:, g * D:(g + 1) * D])
            parts.append(down[g * D:(g + 1) * D])

    heads(w, QA, KA, VA, 4)
    parts.append(x["w_out_ab_2"][0])
    mlp(x["w_up_2"][0], x["w_down_2"][0])
    heads(x["w_in_c_2"][0], 0, D, 2 * D, 8)
    parts.append(x["w_out_c_2"][0])
    mlp(x["w_up_2"][1], x["w_down_2"][1])
    whole = tiles(np.concatenate(parts, 1))
    assert whole.shape[0] in (N_TILES, N_TILES - 1), whole.shape
    if whole.shape[0] < N_TILES:
        whole = np.concatenate([whole, np.zeros((1,) + whole.shape[1:], whole.dtype)], 0)
    return whole


def parameters(x):
    def c(a):
        return np.asarray(a).reshape(-1, P).T
    cols = [x["norm_g"][0], x["final_norm_g"], x["g_mix_2"][0], x["g_ffn_2"][0], x["g_mix_2"][1], x["g_ffn_2"][1],
            x["conv_w"][0, 0], x["conv_w"][0, 1], x["conv_w"][0, 2], x["conv_b"][0], x["gq_a_2"][0], x["gk_a_2"][0],
            x["g_gla_2"][0], x["gq_c_2"][0], x["gk_c_2"][0], x["b_gate_2"][0]]
    return np.ascontiguousarray(np.concatenate([c(a) for a in cols], 1))


def rotary(head):
    rot = head // 4
    half = rot // 2
    inv = np.power(np.float32(500000.0), -np.arange(half, dtype=np.float32) * np.float32(2.0) / np.float32(rot))
    ang = (np.arange(S, dtype=np.float32)[:, None] * inv.astype(np.float32)[None, :]).T
    cos, sin, swap = np.ones((P, S), np.float32), np.zeros((P, S), np.float32), np.zeros((P, P), np.float32)
    for b in range(0, P, head):
        for j in range(half):
            cos[b + j] = cos[b + half + j] = np.cos(ang[j])
            sin[b + j] = sin[b + half + j] = np.sin(ang[j])
            swap[b + half + j, b + j] = -1.0
            swap[b + j, b + half + j] = 1.0
    return cos, sin, swap


def constants():
    small = np.zeros((P, NSMALL), np.float32)
    ca, sa, pa = rotary(128)
    ci, si, pi = rotary(64)
    i, j = np.arange(P)[:, None], np.arange(P)[None, :]
    small[:, C_ID:C_ID + P] = np.eye(P)
    small[:, C_P:C_P + P] = pi
    small[:, C_GM:C_GM + P] = (i <= j) & (i // CH == j // CH)
    earlier = np.where(j < i, 0.0, NEG).astype(np.float32)
    return small, np.concatenate([pa, earlier], 1), np.stack([ca, sa, ci, si])


def kernel(**inputs):
    import concourse.bacc as bacc
    from concourse.bass_utils import run_bass_kernel_spmd

    x = {k: np.asarray(a) for k, a in inputs.items()}
    small, swap, tables = constants()
    near = np.minimum(P + np.arange(P)[:, None] - np.arange(2 * P)[None, :], P) + P
    arrays = {
        "xT": np.ascontiguousarray(x["x"][0].T), "wst": weight_stream(x), "par_d": parameters(x),
        "wg_d": np.ascontiguousarray(x["w_gate_up_2"][0]), "rb_d": np.ascontiguousarray(x["rel_bias"][0][:, near]),
        "small_d": small, "swap_d": swap, "tab_d": tables,
    }
    nc = bacc.Bacc("TRN2", target_bir_lowering=False, num_devices=1)
    args = [nc.dram_tensor(n, a.shape, mybir.dt.from_np(a.dtype), kind="ExternalInput").ap()
            for n, a in arrays.items()]
    out = nc.dram_tensor("outT", (D, S), F, kind="ExternalOutput").ap()
    build(nc, *args, out)
    r = run_bass_kernel_spmd(nc, [arrays], core_ids=[0])
    return np.ascontiguousarray(r.results[0]["outT"].T)[None]
```
